# Optimizing a Trainium2 kernel written in Bass

```python
import math
import jax, jax.numpy as jnp
from jax import lax
import numpy as np

D_MODEL = 2048
BATCH = 1
SEQ = 256
DEPTH = 1

CHUNK = 64
Q_BLOCK = 128
D_MIX = D_MODEL
M_HEADS = 4
M_DV = D_MIX // 2 // M_HEADS
M_DQK = M_DV // 2
M_QK = 2 * M_HEADS * M_DQK
CONV_W = 4
A_HEADS = 4
A_DV = D_MIX // 2 // A_HEADS
A_DQK = A_DV // 2
D_FF = -(-8 * D_MODEL // (3 * 256)) * 256
RMS_EPS = 1e-6
NEG = -1e30
IN_SIZES = (M_QK, M_HEADS * M_DV, M_HEADS * M_DV, M_HEADS, M_HEADS,
            A_HEADS * 2 * A_DQK, A_HEADS * 2 * A_DQK, A_HEADS * A_DV)
N_IN = sum(IN_SIZES)

kernel_name = 'hymba_mlstm_diffattn_block'

def rms_norm(x, g):
    xf = x.astype(jnp.float32)
    y = xf * lax.rsqrt(jnp.mean(xf * xf, axis=-1, keepdims=True) + RMS_EPS)
    return (y * g.astype(jnp.float32)).astype(x.dtype)

def causal_dwconv(x, w, b):
    c = x.shape[-1]
    y = lax.conv_general_dilated(x, w[:, None, :].astype(x.dtype), window_strides=(1,),
                                 padding=[(CONV_W - 1, 0)],
                                 dimension_numbers=('NWC', 'WIO', 'NWC'),
                                 feature_group_count=c)
    return y + b.astype(x.dtype)

def mlstm_chunkwise(q, k, v, i_pre, f_pre):
    B, H, S, dqk = q.shape
    dv = v.shape[-1]
    L = CHUNK
    NC = S // L
    f32 = jnp.float32
    qc = q.astype(f32).reshape(B, H, NC, L, dqk)
    kc = k.astype(f32).reshape(B, H, NC, L, dqk)
    vc = v.astype(f32).reshape(B, H, NC, L, dv)
    log_f = jax.nn.log_sigmoid(f_pre).reshape(B, H, NC, L)
    log_i = i_pre.reshape(B, H, NC, L)
    b = jnp.cumsum(log_f, axis=-1)
    g = b[..., -1]
    a = g[..., None] - b + log_i
    m_loc = jnp.max(a, axis=-1)
    w_loc = jnp.exp(a - m_loc[..., None])
    C_loc = jnp.einsum('bhcs,bhcsv,bhcsk->bhcvk', w_loc, vc, kc)
    n_loc = jnp.einsum('bhcs,bhcsk->bhck', w_loc, kc)

    def step(carry, inp):
        C, n, m = carry
        g_c, m_c, C_c, n_c = inp
        m_new = jnp.maximum(g_c + m, m_c)
        s_old = jnp.exp(g_c + m - m_new)
        s_loc = jnp.exp(m_c - m_new)
        C_new = s_old[..., None, None] * C + s_loc[..., None, None] * C_c
        n_new = s_old[..., None] * n + s_loc[..., None] * n_c
        return (C_new, n_new, m_new), (C, n, m)

    init = (jnp.zeros((B, H, dv, dqk), f32), jnp.zeros((B, H, dqk), f32),
            jnp.full((B, H), NEG, f32))
    xs = (jnp.moveaxis(g, 2, 0), jnp.moveaxis(m_loc, 2, 0),
          jnp.moveaxis(C_loc, 2, 0), jnp.moveaxis(n_loc, 2, 0))
    _, (C_prev, n_prev, m_prev) = lax.scan(step, init, xs)
    C_prev = jnp.moveaxis(C_prev, 0, 2)
    n_prev = jnp.moveaxis(n_prev, 0, 2)
    m_prev = jnp.moveaxis(m_prev, 0, 2)

    causal = jnp.tril(jnp.ones((L, L), dtype=bool))
    D = b[..., :, None] - b[..., None, :] + log_i[..., None, :]
    D = jnp.where(causal, D, NEG)
    inter_log = b + m_prev[..., None]
    m_t = jnp.maximum(inter_log, jnp.max(D, axis=-1))
    W = jnp.exp(D - m_t[..., None]) * jnp.einsum('bhctk,bhcsk->bhcts', qc, kc)
    s_inter = jnp.exp(inter_log - m_t)
    num = (jnp.einsum('bhcts,bhcsv->bhctv', W, vc)
           + s_inter[..., None] * jnp.einsum('bhcvk,bhctk->bhctv', C_prev, qc))
    den = W.sum(-1) + s_inter * jnp.einsum('bhck,bhctk->bhct', n_prev, qc)
    h = num / jnp.maximum(jnp.abs(den), jnp.exp(-m_t))[..., None]
    return h.reshape(B, H, S, dv).astype(v.dtype)

def diff_attention(q, k, v, lam):
    B, H, _, S, d = q.shape
    dv = v.shape[-1]
    nqb = S // Q_BLOCK
    scale = d ** -0.5
    k_chunk = jnp.arange(S) // CHUNK
    vf = v.astype(jnp.float32)
    qb = jnp.moveaxis(q.reshape(B, H, 2, nqb, Q_BLOCK, d), 3, 0)

    def block(args):
        q_blk, blk = args
        s = jnp.einsum('bhcqd,bhckd->bhcqk', q_blk, k).astype(jnp.float32) * scale
        q_chunk = (blk * Q_BLOCK + jnp.arange(Q_BLOCK)) // CHUNK
        mask = k_chunk[None, :] <= q_chunk[:, None]
        p = jax.nn.softmax(jnp.where(mask, s, NEG), axis=-1)
        attn = p[:, :, 0] - lam * p[:, :, 1]
        return jnp.einsum('bhqk,bhkv->bhqv', attn, vf)

    out = lax.map(block, (qb, jnp.arange(nqb)))
    return jnp.moveaxis(out, 0, 2).reshape(B, H, S, dv).astype(v.dtype)

def mixer(h, layer_idx, w_in, conv_w, conv_b, i_bias, f_bias, m_norm_w, q_norm_w, k_norm_w,
          lambda_q1, lambda_k1, lambda_q2, lambda_k2, a_norm_w, w_out):
    B, S, _ = h.shape
    f32 = jnp.float32
    split_idx = np.cumsum(IN_SIZES)[:-1].tolist()
    proj = h @ w_in
    m_qk, m_v, m_o, m_i, m_f, a_q, a_k, a_v = jnp.split(proj, split_idx, axis=-1)

    def heads(t, d):
        return t.reshape(B, S, -1, d).transpose(0, 2, 1, 3)

    m_qk = jax.nn.silu(causal_dwconv(m_qk, conv_w, conv_b))
    m_q, m_k = jnp.split(m_qk, 2, axis=-1)
    m_q = heads(m_q, M_DQK)
    m_k = heads(m_k, M_DQK) * (M_DQK ** -0.5)
    m_v = heads(m_v, M_DV)
    i_pre = (m_i.astype(f32) + i_bias.astype(f32)).transpose(0, 2, 1)
    f_pre = (m_f.astype(f32) + f_bias.astype(f32)).transpose(0, 2, 1)
    hm = mlstm_chunkwise(m_q, m_k, m_v, i_pre, f_pre)
    hm = rms_norm(hm.transpose(0, 2, 1, 3), m_norm_w).reshape(B, S, -1) * jax.nn.sigmoid(m_o)

    a_q = rms_norm(a_q.reshape(B, S, A_HEADS, 2, A_DQK), q_norm_w).transpose(0, 2, 3, 1, 4)
    a_k = rms_norm(a_k.reshape(B, S, A_HEADS, 2, A_DQK), k_norm_w).transpose(0, 2, 3, 1, 4)
    a_v = heads(a_v, A_DV)
    lam_init = 0.8 - 0.6 * math.exp(-0.3 * layer_idx)
    lam = (jnp.exp(jnp.sum(lambda_q1.astype(f32) * lambda_k1.astype(f32)))
           - jnp.exp(jnp.sum(lambda_q2.astype(f32) * lambda_k2.astype(f32))) + lam_init)
    ha = diff_attention(a_q, a_k, a_v, lam)
    ha = (rms_norm(ha.transpose(0, 2, 1, 3), a_norm_w) * (1.0 - lam_init)).reshape(B, S, -1)

    return jnp.concatenate([hm, ha.astype(hm.dtype)], axis=-1) @ w_out

def swiglu(h, w_gate, w_up, w_down):
    return (jax.nn.silu(h @ w_gate) * (h @ w_up)) @ w_down

def setup_inputs(seed: int = 0) -> dict:
    key = jax.random.key(seed)
    ks = jax.random.split(key, 20)
    f32 = jnp.float32

    def nrm(k, shape, scale):
        return jax.random.normal(k, shape, f32) * scale

    return {
        'x': nrm(ks[0], (BATCH, SEQ, D_MODEL), 1.0),
        'norm1_w': 1.0 + nrm(ks[1], (DEPTH, D_MODEL), 0.02),
        'w_in': nrm(ks[2], (DEPTH, D_MODEL, N_IN), D_MODEL ** -0.5),
        'conv_w': nrm(ks[3], (DEPTH, CONV_W, M_QK), CONV_W ** -0.5),
        'conv_b': nrm(ks[4], (DEPTH, M_QK), 0.02),
        'i_bias': nrm(ks[5], (DEPTH, M_HEADS), 0.1),
        'f_bias': jnp.linspace(3.0, 6.0, M_HEADS, dtype=f32)[None, :] + nrm(ks[6], (DEPTH, M_HEADS), 0.1),
        'm_norm_w': 1.0 + nrm(ks[7], (DEPTH, M_HEADS, M_DV), 0.02),
        'q_norm_w': 1.0 + nrm(ks[8], (DEPTH, A_DQK), 0.02),
        'k_norm_w': 1.0 + nrm(ks[9], (DEPTH, A_DQK), 0.02),
        'lambda_q1': nrm(ks[10], (DEPTH, A_DQK), 0.1),
        'lambda_k1': nrm(ks[11], (DEPTH, A_DQK), 0.1),
        'lambda_q2': nrm(ks[12], (DEPTH, A_DQK), 0.1),
        'lambda_k2': nrm(ks[13], (DEPTH, A_DQK), 0.1),
        'a_norm_w': 1.0 + nrm(ks[14], (DEPTH, A_HEADS, A_DV), 0.02),
        'w_out': nrm(ks[15], (DEPTH, D_MIX, D_MODEL), D_MIX ** -0.5),
        'norm2_w': 1.0 + nrm(ks[16], (DEPTH, D_MODEL), 0.02),
        'w_gate': nrm(ks[17], (DEPTH, D_MODEL, D_FF), D_MODEL ** -0.5),
        'w_up': nrm(ks[18], (DEPTH, D_MODEL, D_FF), D_MODEL ** -0.5),
        'w_down': nrm(ks[19], (DEPTH, D_FF, D_MODEL), D_FF ** -0.5),
    }

def reference(x, norm1_w, w_in, conv_w, conv_b, i_bias, f_bias, m_norm_w, q_norm_w, k_norm_w,
              lambda_q1, lambda_k1, lambda_q2, lambda_k2, a_norm_w, w_out, norm2_w,
              w_gate, w_up, w_down):
    for l in range(DEPTH):
        h = rms_norm(x, norm1_w[l])
        x = x + mixer(h, l, w_in[l], conv_w[l], conv_b[l], i_bias[l], f_bias[l], m_norm_w[l],
                      q_norm_w[l], k_norm_w[l], lambda_q1[l], lambda_k1[l], lambda_q2[l],
                      lambda_k2[l], a_norm_w[l], w_out[l])
        h = rms_norm(x, norm2_w[l])
        x = x + swiglu(h, w_gate[l], w_up[l], w_down[l])
    return x


_drawn_inputs = setup_inputs


def setup_inputs(seed=0):
    import zlib

    import numpy as np

    out = dict(_drawn_inputs(seed))
    spreads = {}
    factors = {'conv_b': 8.0,
     'i_bias': 8.0,
     'm_norm_w': 8.0,
     'q_norm_w': 4.743,
     'k_norm_w': 4.469,
     'a_norm_w': 5.546,
     'norm2_w': 4.558}
    for name, (base, spread) in spreads.items():
        noise = np.random.default_rng([zlib.crc32(name.encode()), seed]).standard_normal(out[name].shape)
        drawn = base * np.exp(spread * noise) if base else spread * noise
        out[name] = __import__('jax').numpy.asarray(drawn.astype(out[name].dtype))
    for name, factor in factors.items():
        out[name] = (out[name] * factor).astype(out[name].dtype)
    return out
```

```python
import math
from contextlib import ExitStack

import numpy as np

import concourse.bass as bass
from concourse import mybir

F32 = mybir.dt.float32
F32R = mybir.dt.float32r
ALU = mybir.AluOpType
ACT = mybir.ActivationFunctionType
AX = mybir.AxisListType

P = 128
SEQ = 256
TT = SEQ // P
D = 2048
KT = D // P
D_FF = 5632
KF = D_FF // P
NG = 512
CH = 2 * NG
HEADS = 4
DQK = 128
DV = 256
CONV_W = 4
EPS = 1e-6
NEG = -1e30
LAM_INIT = 0.8 - 0.6 * math.exp(-0.3 * 0)
SCALE = DQK ** -0.5
RAW = 4
SPLIT = 4

C_MQK, C_MV, C_MO, C_IF = 0, 1024, 2048, 3072
C_AQ, C_AK, C_AV = 3080, 4104, 5128
G_AQ, G_AK, G_AV, G_MQ, G_MK, G_MV, G_MO = 0, 2, 4, 6, 7, 8, 10
IN_COLS = [C_AQ + NG * g for g in range(6)] + [NG * g for g in range(6)]
GC = KT // 2
IN_CHUNKS = len(IN_COLS) * GC
OUT0 = IN_CHUNKS
OUT_GROUPS = D // NG
FF0 = OUT0 + OUT_GROUPS * GC
FF_SLICES = D_FF // NG
FF_CHUNKS = 2 * GC
DOWN0 = FF0 + FF_SLICES * FF_CHUNKS
DOWN_CHUNKS = KF

R_N1, R_N2, R_MN, R_AN, R_CW, R_CB, R_QN, R_KN, R_LAM = 0, 16, 32, 40, 48, 80, 88, 89, 90
N_PAR = 94

AT_GATES, AT_ROWS, AT_COLS = 14, 18, 28
AT_SCORE = [39 + 5 * h for h in range(HEADS)]
AT_PT = [p + 3 for p in AT_SCORE]
AT_PV = [p + 4 for p in AT_SCORE]
AT_Y = [p + 6 for p in AT_SCORE]
AT_MS = [73 + 4 * h for h in range(HEADS)]
AT_MPV = [p + 3 for p in AT_MS]
AT_MY = [93, 99]
LAG = 3


def hybrid_block_kernel(nc, x, norm1_w, w_in, conv_w, conv_b, i_bias, f_bias, m_norm_w, q_norm_w,
                        k_norm_w, lambda_q1, lambda_k1, lambda_q2, lambda_k2, a_norm_w, w_out,
                        norm2_w, w_gate, w_up, w_down, out):
    ctx = ExitStack()
    with ctx:
        def sb(name, shape, dt=F32, stack=ctx, parts=P):
            return stack.enter_context(nc.sbuf_tensor(name, [parts] + shape, dt))

        def sem(name):
            return ctx.enter_context(nc.semaphore(name))

        res = sb("res", [TT, D])
        act_hi = sb("act_hi", [KT, SEQ], F32R)
        act_lo = sb("act_lo", [KT, SEQ], F32R)
        w_raw = sb("w_raw", [RAW, CH])
        w_hi = sb("w_hi", [SPLIT, CH], F32R)
        w_lo = sb("w_lo", [SPLIT, CH], F32R)
        stage = sb("stage", [TT, NG])
        scaled = sb("scaled", [TT, NG])
        gated = sb("gated", [TT, NG])
        ident = sb("ident", [P])
        par = sb("par", [N_PAR])
        small = sb("small", [160])
        ss_x = small[:, 0:8].rearrange("p (t b) -> p t b", t=TT)
        ss_x1 = small[:, 8:16].rearrange("p (t b) -> p t b", t=TT)
        tot = small[:, 16:18]
        root = small[:, 18:20]
        r1 = small[:, 20:22]
        r1sq = small[:, 22:24]
        r2 = small[:, 24:26]
        qk_ss = small[:, 26:34]
        qk_v = small[:, 34:42]
        qk_root = small[:, 42:50]
        qk_f = small[:, 50:58]
        eps = small[:, 58:59]
        lam_prod = small[:, 59:61]
        lam_exp = small[:, 61:63]
        neg_lam = small[:, 63:64]
        a_max = small[:, 64:68]
        a_nmax = small[:, 68:72]
        a_sum = small[:, 72:76]
        a_rec = small[:, 76:80]
        a_mix = small[:, 80:82]
        y_ss = small[:, 82:84]
        y_root = small[:, 84:86]
        y_rec = small[:, 86:88]
        y_f = small[:, 88:90]
        a_col = small[:, 90:98]
        exp_nm = small[:, 98:106]
        m_ss = small[:, 106:114]
        m_den = small[:, 114:122]
        m_rec = small[:, 122:130]
        m_v = small[:, 130:138]
        m_v2 = small[:, 138:146]
        m_root = small[:, 146:154]
        one_col = small[:, 154:155]

        mix = ExitStack()
        y_hi = sb("y_hi", [KT, SEQ], F32R, mix)
        y_lo = sb("y_lo", [KT, SEQ], F32R, mix)
        mv = sb("mv", [TT, HEADS, DV + 1], F32, mix)
        probs = sb("probs", [2, P + SEQ], F32, mix)
        a_tmp = sb("a_tmp", [P + SEQ], F32, mix)
        a_mat = sb("a_mat", [P + SEQ], F32, mix)
        a_turn = sb("a_turn", [P + SEQ], F32, mix)
        m_arg = sb("m_arg", [P + SEQ], F32, mix)
        m_exp = sb("m_exp", [P + SEQ], F32, mix)
        m_w = sb("m_w", [P + SEQ], F32, mix)
        causal = sb("causal", [SEQ], F32, mix)
        chunk_mask = sb("chunk_mask", [2, 64], F32, mix)
        ones = sb("ones", [P], F32, mix)
        par_rows = sb("par_rows", [P], F32, mix, N_PAR)
        w_if = sb("w_if", [KT, 8], F32, mix)
        w_if_hi = sb("w_if_hi", [KT, 8], F32R, mix)
        w_if_lo = sb("w_if_lo", [KT, 8], F32R, mix)
        gate_cols = sb("gate_cols", [TT, 8], F32, mix)
        select = sb("select", [HEADS, P], F32, mix, HEADS)
        bias_if = sb("bias_if", [2], F32, mix, HEADS)
        zero_row = sb("zero_row", [SEQ], F32, mix, HEADS)
        f_pre = sb("f_pre", [SEQ], F32, mix, HEADS)
        f_abs = sb("f_abs", [SEQ], F32, mix, HEADS)
        f_exp = sb("f_exp", [SEQ], F32, mix, HEADS)
        f_ln = sb("f_ln", [SEQ], F32, mix, HEADS)
        log_f = sb("log_f", [SEQ], F32, mix, HEADS)
        f_sum = sb("f_sum", [SEQ], F32, mix, HEADS)
        a_row = sb("a_row", [SEQ], F32, mix, HEADS)
        m_run = sb("m_run", [SEQ], F32, mix, HEADS)
        neg_run = sb("neg_run", [SEQ], F32, mix, HEADS)
        neg_m = sb("neg_m", [SEQ], F32, mix, HEADS)
        attn = ExitStack()
        aq = sb("aq", [2 * HEADS, SEQ], F32, attn)
        ak = sb("ak", [2 * HEADS, SEQ], F32, attn)
        av = sb("av", [TT, HEADS * DV], F32, attn)
        attn.close()
        lstm = ExitStack()
        conv = sb("conv", [HEADS, SEQ], F32, lstm)
        mq = sb("mq", [HEADS, SEQ], F32, lstm)
        mk = sb("mk", [HEADS, SEQ], F32, lstm)
        m_num = sb("m_num", [TT, HEADS, DV + 1], F32, lstm)
        lstm.close()
        mix.close()
        ff = ExitStack()
        hid_hi = sb("hid_hi", [KF, SEQ], F32R, ff)
        hid_lo = sb("hid_lo", [KF, SEQ], F32R, ff)
        ff.close()

        acc = [ctx.enter_context(nc.psum_tensor(f"acc{i}", [P, NG], F32)) for i in range(4)]
        aux = [ctx.enter_context(nc.psum_tensor(f"aux{i}", [P, NG], F32)) for i in range(4)]

        raw_landed = [sem(f"raw_landed{s}") for s in range(RAW)]
        hi_done = sem("hi_done")
        lo_done = sem("lo_done")
        chunk_used = sem("chunk_used")
        acc_free = sem("acc_free")
        x_landed = [sem(f"x_landed{b}") for b in range(4)]
        par_landed = sem("par_landed")
        wif_landed = sem("wif_landed")
        bias_landed = sem("bias_landed")
        zeroed = sem("zeroed")
        const_ready = sem("const_ready")
        par_turned = sem("par_turned")
        par_ready = sem("par_ready")
        turned = sem("turned")
        scaled_ready = sem("scaled_ready")
        turn_hi = sem("turn_hi")
        turn_lo = sem("turn_lo")
        x_squared = sem("x_squared")
        x_tot = sem("x_tot")
        x_root = sem("x_root")
        r1_ready = sem("r1_ready")
        wif_hi = sem("wif_hi")
        wif_lo = sem("wif_lo")
        squared = sem("squared")
        qk_var = sem("qk_var")
        qk_rooted = sem("qk_rooted")
        stage_ready = sem("stage_ready")
        qk_turned = sem("qk_turned")
        qk_out = sem("qk_out")
        av_ready = sem("av_ready")
        gates_done = sem("gates_done")
        gates_read = sem("gates_read")
        lam_exped = sem("lam_exped")
        lam_read = sem("lam_read")
        rows_turned = sem("rows_turned")
        f_ready = sem("f_ready")
        ln_ready = sem("ln_ready")
        rows_ready = sem("rows_ready")
        cols_turned = sem("cols_turned")
        cols_read = sem("cols_read")
        scored = sem("scored")
        maxed = sem("maxed")
        exped = sem("exped")
        mat_ready = sem("mat_ready")
        mat_turned = sem("mat_turned")
        mat_out = sem("mat_out")
        pv_done = sem("pv_done")
        y_squared = sem("y_squared")
        y_scaled = sem("y_scaled")
        y_turned = sem("y_turned")
        y_mul = sem("y_mul")
        y_hi_done = sem("y_hi_done")
        y_lo_done = sem("y_lo_done")
        m_turned = sem("m_turned")
        conv_first = sem("conv_first")
        conv_done = sem("conv_done")
        silu_done = sem("silu_done")
        mv_ready = sem("mv_ready")
        m_scored = sem("m_scored")
        m_masked = sem("m_masked")
        m_exped = sem("m_exped")
        mw_ready = sem("mw_ready")
        mpv_done = sem("mpv_done")
        mnum_read = sem("mnum_read")
        msq_done = sem("msq_done")
        m_var = sem("m_var")
        m_rooted = sem("m_rooted")
        sig_done = sem("sig_done")
        x1_ready = sem("x1_ready")
        x1_squared = sem("x1_squared")
        x1_tot = sem("x1_tot")
        x1_root = sem("x1_root")
        r2_ready = sem("r2_ready")
        gate_act = sem("gate_act")
        hid_ready = sem("hid_ready")
        hid_turned = sem("hid_turned")
        hid_hi_done = sem("hid_hi_done")
        hid_lo_done = sem("hid_lo_done")
        bank_done = sem("bank_done")
        out_ready = sem("out_ready")
        out_stored = sem("out_stored")
        act_step = sem("act_step")
        dve_step = sem("dve_step")

        def tiles(w):
            return w[0].rearrange("(k p) n -> p k n", p=P)

        win_t, wout_t, wgate_t, wup_t, wdown_t = (tiles(w) for w in (w_in, w_out, w_gate, w_up, w_down))
        x_t = x[0].rearrange("(t p) n -> p t n", p=P)
        out_t = out[0].rearrange("(t p) n -> p t n", p=P)

        block = ctx.enter_context(nc.Block())

        @block.sync
        def _(sp):
            def load(n, src, slot, wait=True):
                if wait:
                    sp.wait_ge(lo_done, n - (RAW - 1))
                dst = w_raw[:, slot, :].rearrange("p (k n) -> p k n", k=src.shape[1])
                sp.dma_start(dst, src).then_inc(raw_landed[slot], 16)

            for g, col in enumerate(IN_COLS):
                for c in range(GC):
                    if g == 0 and c < 4:
                        sp.dma_start(res[:, :, NG * c:NG * (c + 1)],
                                     x_t[:, :, NG * c:NG * (c + 1)]).then_inc(x_landed[c], 16)
                    load(g * GC + c, win_t[:, 2 * c:2 * c + 2, col:col + NG], c % RAW, g * GC + c >= RAW)
            with sp.Fori(1, OUT_GROUPS + 1) as g:
                for c in range(GC):
                    k = (2 * c + KT // 2) % KT
                    load(g * GC + (OUT0 - GC + c), wout_t[:, k:k + 2, bass.ds(g * NG - NG, NG)], c % RAW)
            with sp.Fori(1, FF_SLICES + 1) as i:
                for c in range(FF_CHUNKS):
                    w = wgate_t if c < GC else wup_t
                    k = 2 * (c % GC)
                    load(i * FF_CHUNKS + (FF0 - FF_CHUNKS + c), w[:, k:k + 2, bass.ds(i * NG - NG, NG)], c % RAW)
            with sp.Fori(1, 3) as p:
                for k in range(DOWN_CHUNKS):
                    load(p * DOWN_CHUNKS + (DOWN0 - DOWN_CHUNKS + k), wdown_t[:, k:k + 1, bass.ds(p * CH - CH, CH)],
                         k % RAW)
            for j in range(8):
                col, t = NG * (j // 2), j % 2
                sp.wait_ge(out_ready, j + 1)
                sp.dma_start(out_t[:, t, col:col + NG], res[:, t, col:col + NG]).then_inc(out_stored, 16)
            sp.wait_ge(out_stored, 16 * 8)

        @block.gpsimd
        def _(pool):
            pool.memset(ident[:], 0.0).then_inc(zeroed, 1)
            pool.memset(causal[:], 0.0).then_inc(zeroed, 1)
            pool.memset(chunk_mask[:], 0.0).then_inc(zeroed, 1)
            pool.memset(select[:], 0.0).then_inc(zeroed, 1)
            pool.memset(ones[:], 1.0).then_inc(const_ready, 1)
            pool.memset(zero_row[:], 0.0).then_inc(const_ready, 1)
            pool.memset(mv[:, :, :, DV:DV + 1], 1.0).then_inc(const_ready, 1)
            pool.memset(eps, EPS).then_inc(const_ready, 1)
            pool.memset(one_col, 1.0).then_inc(const_ready, 1)
            pool.wait_ge(zeroed, 4)
            pool.affine_select(out=ident[:], in_=ident[:], compare_op=ALU.not_equal, fill=1.0, base=0,
                               pattern=[[-1, P]], channel_multiplier=1).then_inc(const_ready, 1)
            pool.affine_select(out=causal[:, 0:P], in_=causal[:, 0:P], compare_op=ALU.is_ge, fill=NEG,
                               base=0, pattern=[[1, P]], channel_multiplier=-1).then_inc(const_ready, 1)
            pool.affine_select(out=chunk_mask[:], in_=chunk_mask[:], compare_op=ALU.is_ge, fill=NEG,
                               base=-64, pattern=[[0, 2], [0, 64]], channel_multiplier=1).then_inc(const_ready, 1)
            pool.affine_select(out=select[:], in_=select[:], compare_op=ALU.not_equal, fill=1.0, base=0,
                               pattern=[[-1, HEADS], [0, P]], channel_multiplier=1).then_inc(const_ready, 1)

        CONSTS = 9

        @block.tensor
        def _(pe):
            def chunk(n, slot, banks, kts, width, hi, lo, first, last, by_bank=False):
                pe.wait_ge(lo_done, n + 1)
                for j in range(width):
                    for kk, k in enumerate(kts):
                        cols = slice(NG * (kk * width + j), NG * (kk * width + j + 1))
                        for t in range(TT):
                            tok = slice(P * t, P * (t + 1))
                            bank = banks[t][j]
                            pe.matmul(bank[:], hi[:, k, tok], w_lo[:, slot, cols],
                                      start=first and kk == 0, stop=False)
                            pe.matmul(bank[:], lo[:, k, tok], w_hi[:, slot, cols], start=False, stop=False)
                            mm = pe.matmul(bank[:], hi[:, k, tok], w_hi[:, slot, cols], start=False,
                                           stop=last and kk == len(kts) - 1)
                            if by_bank:
                                mm.then_inc(bank_done, 1)
                if not by_bank:
                    mm.then_inc(chunk_used, 1)

            def turn(src, banks, done):
                for t in range(TT):
                    for b in range(4):
                        mm = pe.transpose(banks[t][:, P * b:P * (b + 1)], src[:, t, P * b:P * (b + 1)], ident[:])
                mm.then_inc(done, 1)

            def turn_x(b):
                pe.wait_ge(x_landed[b], 16)
                if b >= 2:
                    pe.wait_ge(turn_lo, 2 * (b - 1))
                turn(res[:, :, NG * b:NG * (b + 1)], aux[2 * (b % 2):2 * (b % 2) + 2], turned)

            def gates():
                pe.wait_ge(wif_lo, 1)
                pe.wait_ge(turn_lo, 8)
                for t in range(TT):
                    o = aux[2][:, 8 * t:8 * t + 8]
                    for k in range(KT):
                        a, b = act_hi[:, k, P * t:P * (t + 1)], act_lo[:, k, P * t:P * (t + 1)]
                        pe.matmul(o, a, w_if_lo[:, k, :], start=(k == 0), stop=False)
                        pe.matmul(o, b, w_if_hi[:, k, :], start=False, stop=False)
                        pe.matmul(o, a, w_if_hi[:, k, :], start=False, stop=(k == KT - 1))
                pe.matmul(aux[2][:, 16:18], ones[:], lam_prod, start=True, stop=True).then_inc(gates_done, 1)

            def gate_rows():
                pe.wait_ge(gates_read, 1)
                for j in range(2):
                    for t in range(TT):
                        mm = pe.transpose(aux[3][0:HEADS, SEQ * j + P * t:SEQ * j + P * (t + 1)],
                                          gate_cols[:, t, HEADS * j:HEADS * (j + 1)], ident[:])
                mm.then_inc(rows_turned, 1)

            def gate_columns():
                pe.wait_ge(rows_ready, 1)
                pe.wait_ge(lam_read, 1)
                for j, row in enumerate((a_row, neg_m)):
                    for t in range(TT):
                        o = 8 * j + 4 * t
                        mm = pe.transpose(aux[2][:, o:o + 4], row[:, P * t:P * (t + 1)], ident[0:4, 0:4])
                mm.then_inc(cols_turned, 1)

            def scores(h):
                if h == 0:
                    pe.wait_ge(qk_out, 8)
                else:
                    pe.wait_ge(exped, h)
                for c in range(2):
                    b = 2 * h + c
                    pe.matmul(aux[1][:, P * c:P * (c + 1)], aq[:, b, 0:P], ak[:, b, 0:P], start=True, stop=True)
                    mm = pe.matmul(aux[0][:, SEQ * c:SEQ * (c + 1)], aq[:, b, P:SEQ], ak[:, b, :],
                                   start=True, stop=True)
                mm.then_inc(scored, 1)

            def turn_mat(h):
                pe.wait_ge(mat_ready, h + 1)
                if h:
                    pe.wait_ge(y_lo_done, h)
                for b in range(3):
                    mm = pe.transpose(aux[2][:, P * b:P * (b + 1)], a_mat[:, P * b:P * (b + 1)], ident[:])
                mm.then_inc(mat_turned, 1)

            def attend(h):
                pe.wait_ge(mat_out, h + 1)
                pe.wait_ge(av_ready, 2 * (h // 2 + 1))
                if h:
                    pe.wait_ge(y_scaled, h)
                v = slice(DV * h, DV * (h + 1))
                pe.matmul(aux[3][:, 0:DV], a_turn[:, 0:P], av[:, 0, v], start=True, stop=True)
                pe.matmul(aux[3][:, DV:2 * DV], a_turn[:, P:2 * P], av[:, 0, v], start=True, stop=False)
                pe.matmul(aux[3][:, DV:2 * DV], a_turn[:, 2 * P:3 * P], av[:, 1, v],
                          start=False, stop=True).then_inc(pv_done, 1)

            def turn_y(h):
                pe.wait_ge(y_scaled, h + 1)
                pe.wait_ge(mat_out, h + 1)
                for b in range(2):
                    for t in range(TT):
                        mm = pe.transpose(aux[2][:, SEQ * b + P * t:SEQ * b + P * (t + 1)],
                                          stage[:, t, P * b:P * (b + 1)], ident[:])
                mm.then_inc(y_turned, 1)

            def turn_mqk(j):
                pe.wait_ge(stage_ready, 10 + 2 * j)
                if j == 0:
                    pe.wait_ge(exped, HEADS)
                else:
                    pe.wait_ge(conv_done, j)
                for b in range(HEADS):
                    for t in range(TT):
                        o = SEQ * (b % 2) + P * t
                        mm = pe.transpose(aux[b // 2][:, o:o + P], stage[:, t, P * b:P * (b + 1)], ident[:])
                mm.then_inc(m_turned, 1)

            def lstm_scores(h):
                if h == 0:
                    pe.wait_ge(silu_done, 2)
                else:
                    pe.wait_ge(mw_ready, h)
                pe.matmul(aux[0][:, 0:SEQ], mk[:, h, 0:P], mq[:, h, :], start=True, stop=True)
                pe.matmul(aux[0][:, SEQ:SEQ + P], mk[:, h, P:SEQ], mq[:, h, P:SEQ], start=True, stop=True)
                pe.matmul(aux[1][:, 0:SEQ], select[:, h, :], neg_run[:], start=True,
                          stop=True).then_inc(m_scored, 1)

            def lstm_attend(h):
                pe.wait_ge(mw_ready, h + 1)
                pe.wait_ge(mv_ready, 2 * (h // 2 + 1))
                if h == 0:
                    pe.wait_ge(y_lo_done, HEADS)
                else:
                    pe.wait_ge(mnum_read, 2 * h)
                    pe.wait_ge(msq_done, h)
                pe.matmul(aux[2][:, 0:DV + 1], m_w[:, 0:P], mv[:, 0, h, :], start=True, stop=True)
                pe.matmul(aux[3][:, 0:DV + 1], m_w[:, P:2 * P], mv[:, 0, h, :], start=True, stop=False)
                pe.matmul(aux[3][:, 0:DV + 1], m_w[:, 2 * P:3 * P], mv[:, 1, h, :], start=False,
                          stop=True).then_inc(mpv_done, 1)

            pe.wait_ge(const_ready, CONSTS)
            pe.wait_ge(par_landed, 16 * 12)
            pe.transpose(aux[3][:, 0:N_PAR], par_rows[:], ident[0:N_PAR, 0:N_PAR]).then_inc(par_turned, 1)
            turn_x(0)
            pe.wait_ge(par_ready, 1)
            turn_x(1)

            for n in range(IN_CHUNKS):
                g, c = n // GC, n % GC
                if c == 0 and g >= 2:
                    pe.wait_ge(acc_free, g - 1)
                if g == 0 and c % 2 == 0:
                    pe.wait_ge(turn_lo, c + 2)
                banks = acc[2 * (g % 2):2 * (g % 2) + 2]
                chunk(n, n % SPLIT, [[b] for b in banks], (2 * c, 2 * c + 1), 1, act_hi, act_lo,
                      c == 0, c == GC - 1)
                if n in (0, 2):
                    turn_x(2 + n // 2)
                if n == AT_GATES:
                    gates()
                if n == AT_ROWS:
                    gate_rows()
                if n == AT_COLS:
                    gate_columns()
                if 1 <= g <= 4 and c == LAG:
                    pe.wait_ge(stage_ready, 2 * g)
                    if g >= 2:
                        pe.wait_ge(qk_out, 2 * (g - 1))
                    turn(stage, aux[0:2], qk_turned)
                for h in range(HEADS):
                    if n == AT_SCORE[h]:
                        scores(h)
                    if n == AT_PT[h]:
                        turn_mat(h)
                    if n == AT_PV[h]:
                        attend(h)
                    if n == AT_Y[h]:
                        turn_y(h)
                    if n == AT_MS[h]:
                        lstm_scores(h)
                    if n == AT_MPV[h]:
                        lstm_attend(h)
                if g in (G_MQ + 1, G_MK + 1) and c == LAG:
                    turn_mqk(g - G_MQ - 1)
                if n == AT_MY[0]:
                    pe.wait_ge(stage_ready, 14)
                    turn(stage, aux[0:2], turned)

            for n in range(OUT0, FF0):
                g, c = divmod(n - OUT0, GC)
                if c == 0:
                    if g < 2:
                        pe.wait_ge(acc_free, len(IN_COLS) - 1 + g)
                    else:
                        pe.wait_ge(x1_ready, 2 * (g - 1))
                if g == 0 and c == 4:
                    pe.wait_ge(turn_lo, 10)
                if g == 0 and c == 6:
                    pe.wait_ge(turn_lo, 12)
                k = (2 * c + KT // 2) % KT
                banks = acc[2 * (g % 2):2 * (g % 2) + 2]
                chunk(n, n % SPLIT, [[b] for b in banks], (k, k + 1), 1, y_hi, y_lo, c == 0, c == GC - 1)
                if n == AT_MY[1]:
                    pe.wait_ge(stage_ready, 16)
                    pe.wait_ge(turn_lo, 10)
                    turn(stage, aux[0:2], turned)
                if g >= 1 and c == LAG:
                    pe.wait_ge(x1_ready, 2 * g)
                    pe.wait_ge(turn_lo, 10 + 2 * g)
                    turn(res[:, :, NG * (g - 1):NG * g], aux[0:2], turned)

            def ff_slice(i, first):
                n = i * FF_CHUNKS + FF0
                for c in range(FF_CHUNKS):
                    if c == 0 and not first:
                        pe.wait_ge(gate_act, i * 2)
                    if c == 0 and first:
                        pe.wait_ge(x1_ready, 6)
                    if c == GC and not first:
                        pe.wait_ge(hid_ready, i * 2)
                    if c == GC and first:
                        pe.wait_ge(x1_ready, 8)
                    if first and c in (0, 2, 4, 6):
                        pe.wait_ge(turn_lo, 14 + c)
                    banks = acc[0:2] if c < GC else acc[2:4]
                    k = 2 * (c % GC)
                    chunk(n + c, c % SPLIT, [[b] for b in banks], (k, k + 1), 1, act_hi, act_lo,
                          c % GC == 0, c % GC == GC - 1)
                    if c == LAG and first:
                        pe.wait_ge(x1_ready, 8)
                        pe.wait_ge(turn_lo, 18)
                        turn(res[:, :, NG * 3:NG * 4], aux[0:2], turned)
                    if c == LAG and not first:
                        turn_hidden(i)

            def turn_hidden(i):
                pe.wait_ge(hid_ready, i * 2)
                if isinstance(i, int):
                    pe.wait_ge(hid_lo_done, i * 2 - 2)
                else:
                    pe.wait_ge(hid_lo_done, i * 2 - 2 + 2 * 0)
                turn(stage, aux[0:2], hid_turned)

            ff_slice(0, True)
            pe.wait_ge(turn_lo, 20)
            with pe.Fori(1, FF_SLICES) as i:
                ff_slice(i, False)

            for p in range(2):
                first_banks = [[acc[0], aux[2]], [acc[1], aux[3]]]
                last_banks = [[acc[2], aux[0]], [acc[3], aux[1]]]
                for k in range(KF):
                    if p == 0 and k == 0:
                        pe.wait_ge(gate_act, 2 * FF_SLICES)
                    if p == 0 and k == KF - 4:
                        pe.wait_ge(hid_lo_done, 2 * FF_SLICES)
                    if p == 0 and k < KF - 4 and k % 4 == 0:
                        pe.wait_ge(hid_lo_done, 2 * (k // 4 + 1))
                    chunk(DOWN0 + p * KF + k, k % SPLIT, last_banks if p else first_banks, (k,), 2,
                          hid_hi, hid_lo, k == 0, k == KF - 1, p == 1 and k == KF - 1)
                    if p == 0 and k == LAG:
                        turn_hidden(FF_SLICES)

        @block.scalar
        def _(act):
            steps = [0]

            def then(ins):
                steps[0] += 1
                ins.then_inc(act_step, 1)
                act.wait_ge(act_step, steps[0])

            def split_hi(n, slot):
                use = (n - slot) // RAW + 1 if isinstance(n, int) else None
                if use is not None:
                    act.wait_ge(raw_landed[slot], 16 * use)
                else:
                    raise NotImplementedError
                if n >= SPLIT:
                    act.wait_ge(chunk_used, n - (SPLIT - 1))
                act.activation(w_hi[:, slot, :], w_raw[:, slot, :], ACT.Copy).then_inc(hi_done, 1)

            def turned_hi(dst, j, wait, t):
                act.wait_ge(scaled_ready, j)
                act.activation(dst, scaled[:, t, :].rearrange("p (k s) -> p k s", k=4),
                               ACT.Copy).then_inc(turn_hi, 1)

            rows = [(norm1_w[0], R_N1), (norm2_w[0], R_N2), (m_norm_w[0].rearrange("h d -> (h d)"), R_MN),
                    (a_norm_w[0].rearrange("h d -> (h d)"), R_AN),
                    (conv_w[0].rearrange("j c -> (j c)"), R_CW), (conv_b[0], R_CB),
                    (q_norm_w[0], R_QN), (k_norm_w[0], R_KN), (lambda_q1[0], R_LAM),
                    (lambda_q2[0], R_LAM + 1), (lambda_k1[0], R_LAM + 2), (lambda_k2[0], R_LAM + 3)]
            for src, r in rows:
                n = src.shape[0] // P
                act.dma_start(par_rows[r:r + n, :], src.rearrange("(r c) -> r c", c=P)).then_inc(par_landed, 16)
            act.dma_start(w_if[:], win_t[:, :, C_IF:C_IF + 8]).then_inc(wif_landed, 16)
            act.dma_start(bias_if[:, 0:1], i_bias[0].rearrange("(h o) -> h o", o=1)).then_inc(bias_landed, 16)
            act.dma_start(bias_if[:, 1:2], f_bias[0].rearrange("(h o) -> h o", o=1)).then_inc(bias_landed, 16)

            def x_hi(b):
                for t in range(TT):
                    turned_hi(act_hi[:, 4 * b:4 * b + 4, P * t:P * (t + 1)], 2 * b + t + 1, None, t)
                for t in range(TT):
                    act.activation(gated[:, t, :], res[:, t, NG * b:NG * (b + 1)], ACT.Square,
                                   accum_out=ss_x[:, t, b:b + 1]).then_inc(x_squared, 1)

            def par_copy():
                act.wait_ge(par_turned, 1)
                act.activation(par[:], aux[3][:, 0:N_PAR], ACT.Copy).then_inc(par_ready, 1)

            def small_work(n):
                g, c = n // GC, n % GC
                if n in (1, 3, 5):
                    x_hi((n + 1) // 2)
                if n == 6:
                    act.wait_ge(x_tot, 1)
                    act.wait_ge(const_ready, CONSTS)
                    act.activation(root, tot, ACT.Sqrt, bias=eps, scale=1.0 / D).then_inc(x_root, 1)
                if n == 7:
                    act.wait_ge(wif_landed, 16)
                    act.activation(w_if_hi[:], w_if[:], ACT.Copy).then_inc(wif_hi, 1)
                if 1 <= g <= 4 and c == LAG - 1:
                    act.wait_ge(chunk_used, g * GC)
                    banks = acc[2 * ((g - 1) % 2):2 * ((g - 1) % 2) + 2]
                    for t in range(TT):
                        act.activation(gated[:, t, :], banks[t][:], ACT.Square).then_inc(squared, 1)
                if 1 <= g <= 4 and c == LAG:
                    act.wait_ge(qk_var, g)
                    act.activation(qk_root, qk_v, ACT.Sqrt, bias=eps).then_inc(qk_rooted, 1)
                if 1 <= g <= 4 and c == 2 * LAG:
                    act.wait_ge(qk_turned, g)
                    dst, w = (aq, R_QN) if g <= 2 else (ak, R_KN)
                    b = 4 * ((g - 1) % 2)
                    for t in range(TT):
                        act.activation(dst[:, b:b + 4, P * t:P * (t + 1)],
                                       aux[t][:].rearrange("p (k s) -> p k s", k=4),
                                       ACT.Copy, scale=par[:, w:w + 1]).then_inc(qk_out, 1)
                if 5 <= g <= 10 and c == LAG - 1:
                    act.wait_ge(chunk_used, g * GC)
                    banks = acc[2 * ((g - 1) % 2):2 * ((g - 1) % 2) + 2]
                    for t in range(TT):
                        if g - 1 < G_MQ:
                            o = NG * (g - 1 - G_AV)
                            dst, src, done = av[:, t, o:o + NG], banks[t][:], av_ready
                        elif g - 1 < G_MV:
                            dst, src, done = stage[:, t, :], banks[t][:], stage_ready
                            act.wait_ge(y_turned, 3 if g - 1 == G_MQ else 4)
                        else:
                            o = 2 * (g - 1 - G_MV)
                            dst = mv[:, t, o:o + 2, 0:DV]
                            src, done = banks[t][:].rearrange("p (h d) -> p h d", h=2), mv_ready
                        act.activation(dst, src, ACT.Copy, scale=r1[:, t:t + 1]).then_inc(done, 1)
                if n == AT_GATES + LAG:
                    act.wait_ge(gates_read, 1)
                    act.activation(lam_exp, aux[2][:, 16:18], ACT.Exp).then_inc(lam_exped, 1)
                if n == AT_ROWS + LAG:
                    act.wait_ge(f_ready, 1)
                    then(act.activation(f_exp[:], f_abs[:], ACT.Exp, scale=-1.0))
                    act.activation(f_ln[:], f_exp[:], ACT.Ln, bias=one_col[0:HEADS, :]).then_inc(ln_ready, 1)
                if n == AT_COLS + LAG:
                    act.wait_ge(cols_read, 1)
                    act.activation(exp_nm, aux[2][:, 8:16], ACT.Exp).then_inc(cols_read, 1)
                for h in range(HEADS):
                    if n == AT_SCORE[h] + LAG:
                        act.wait_ge(maxed, h + 1)
                        if h:
                            act.wait_ge(mat_ready, h)
                        for c in range(2):
                            act.activation(probs[:, c, 0:P], aux[1][:, P * c:P * (c + 1)], ACT.Exp,
                                           bias=a_nmax[:, c:c + 1], scale=SCALE, accum_out=a_sum[:, c:c + 1])
                            e = act.activation(probs[:, c, P:P + SEQ], aux[0][:, SEQ * c:SEQ * (c + 1)], ACT.Exp,
                                               bias=a_nmax[:, 2 + c:3 + c], scale=SCALE,
                                               accum_out=a_sum[:, 2 + c:3 + c])
                        e.then_inc(exped, 1)
                    if n == AT_PT[h] + 1:
                        act.wait_ge(mat_turned, h + 1)
                        if h:
                            act.wait_ge(pv_done, h)
                        act.activation(a_turn[:], aux[2][:, 0:P + SEQ], ACT.Copy).then_inc(mat_out, 1)
                    if n == AT_PV[h] + 2:
                        act.wait_ge(pv_done, h + 1)
                        for t in range(TT):
                            s = act.activation(gated[:, t, 0:DV], aux[3][:, DV * t:DV * (t + 1)], ACT.Square,
                                               accum_out=y_ss[:, t:t + 1])
                        then(s)
                        act.activation(y_root, y_ss, ACT.Sqrt, bias=eps, scale=1.0 / DV).then_inc(y_squared, 1)
                    if n == AT_Y[h] + LAG:
                        act.wait_ge(y_mul, h + 1)
                        act.activation(y_hi[:, 8 + 2 * h:10 + 2 * h, :],
                                       scaled[:, 0, :].rearrange("p (k s) -> p k s", k=2),
                                       ACT.Copy).then_inc(y_hi_done, 1)
                if g in (G_MQ + 1, G_MK + 1) and c == 2 * LAG:
                    j = g - G_MQ - 1
                    act.wait_ge(m_turned, j + 1)
                    if j:
                        act.wait_ge(silu_done, j)
                    for b in range(HEADS):
                        act.activation(conv[:, b, :], aux[b // 2][:, SEQ * (b % 2):SEQ * (b % 2 + 1)],
                                       ACT.Identity, bias=par[:, R_CB + 4 * j + b:R_CB + 4 * j + b + 1],
                                       scale=par[:, R_CW + 24 + 4 * j + b:R_CW + 24 + 4 * j + b + 1]
                                       ).then_inc(conv_first, 1)
                if g in (G_MQ + 1, G_MK + 1) and c == 2 * LAG + 1:
                    j = g - G_MQ - 1
                    act.wait_ge(conv_done, j + 1)
                    act.activation((mk if j else mq)[:], conv[:], ACT.Silu).then_inc(silu_done, 1)
                for h in range(HEADS):
                    if n == AT_MS[h] + LAG:
                        act.wait_ge(m_masked, h + 1)
                        if h:
                            act.wait_ge(mw_ready, h)
                        act.activation(m_exp[:, 0:SEQ], m_arg[:, 0:SEQ], ACT.Exp, bias=a_col[:, h:h + 1])
                        act.activation(m_exp[:, SEQ:SEQ + P], m_arg[:, SEQ:SEQ + P], ACT.Exp,
                                       bias=a_col[:, 4 + h:5 + h]).then_inc(m_exped, 1)
                    if n == AT_MPV[h] + LAG:
                        for t in range(TT):
                            act.wait_ge(mnum_read, 2 * h + t + 1)
                            if h:
                                act.wait_ge(msq_done, h)
                            s = act.activation(gated[:, t, 0:DV], aux[2 + t][:, 0:DV], ACT.Square,
                                               accum_out=m_ss[:, 4 * t + h:4 * t + h + 1])
                        s.then_inc(msq_done, 1)
                if n == AT_MPV[3] + LAG:
                    act.wait_ge(m_var, 1)
                    act.activation(m_root, m_v2, ACT.Sqrt, bias=eps, scale=1.0 / DV).then_inc(m_rooted, 1)
                if n in (AT_MY[0] - 1, AT_MY[1] - 1):
                    j = int(n > AT_MY[0])
                    act.wait_ge(chunk_used, (G_MO + j + 1) * GC)
                    if j:
                        act.wait_ge(stage_ready, 14)
                    for t in range(TT):
                        act.activation(gated[:, t, :], acc[2 * j + t][:], ACT.Sigmoid,
                                       scale=r1[:, t:t + 1]).then_inc(sig_done, 1)
                if n in (AT_MY[0] + LAG, AT_MY[1] + LAG):
                    j = int(n > OUT0)
                    for t in range(TT):
                        turned_hi(y_hi[:, 4 * j:4 * j + 4, P * t:P * (t + 1)], 9 + 2 * j + t, None, t)

            def x1_squares(g):
                act.wait_ge(x1_ready, 2 * g + 2)
                for t in range(TT):
                    s = act.activation(gated[:, t, :], res[:, t, NG * g:NG * (g + 1)], ACT.Square,
                                       accum_out=ss_x1[:, t, g:g + 1])
                s.then_inc(x1_squared, 1)

            def x1_hi(g):
                for t in range(TT):
                    turned_hi(act_hi[:, 4 * g:4 * g + 4, P * t:P * (t + 1)], 13 + 2 * g + t, None, t)

            def hidden_hi(i):
                act.wait_ge(hid_turned, i)
                for t in range(TT):
                    act.activation(hid_hi[:, bass.ds(i * 4 - 4, 4), P * t:P * (t + 1)],
                                   aux[t][:].rearrange("p (k s) -> p k s", k=4), ACT.Copy).then_inc(hid_hi_done, 1)

            def gate(i, first):
                act.wait_ge(chunk_used, i * FF_CHUNKS + (FF0 + GC))
                if not first:
                    act.wait_ge(hid_ready, i * 2)
                for t in range(TT):
                    act.activation(gated[:, t, :], acc[t][:], ACT.Silu, scale=r2[:, t:t + 1]).then_inc(gate_act, 1)

            par_copy()
            x_hi(0)
            for n in range(FF0):
                split_hi(n, n % SPLIT)
                small_work(n)
                if n > OUT0 + GC and (n - OUT0) % GC == LAG - 1:
                    x1_squares((n - OUT0) // GC - 1)
                if n > OUT0 + GC and (n - OUT0) % GC == 2 * LAG:
                    x1_hi((n - OUT0) // GC - 1)

            def ff_slice(i, first):
                for c in range(FF_CHUNKS):
                    act.wait_ge(raw_landed[c % RAW], i * (16 * FF_CHUNKS // RAW) + 16 * ((FF0 + c) // RAW + 1))
                    act.wait_ge(chunk_used, i * FF_CHUNKS + (FF0 + c - (SPLIT - 1)))
                    act.activation(w_hi[:, c % SPLIT, :], w_raw[:, c % RAW, :], ACT.Copy).then_inc(hi_done, 1)
                    if c == LAG - 1 and first:
                        x1_squares(3)
                    if c == 2 * LAG and first:
                        x1_hi(3)
                        act.wait_ge(x1_tot, 1)
                        act.activation(root, tot, ACT.Sqrt, bias=eps, scale=1.0 / D).then_inc(x1_root, 1)
                    if c == 2 * LAG and not first:
                        hidden_hi(i)
                    if c == GC + LAG - 1:
                        if first:
                            act.wait_ge(r2_ready, 1)
                        gate(i, first)

            ff_slice(0, True)
            with act.Fori(1, FF_SLICES) as i:
                ff_slice(i, False)
            for n in range(DOWN0, DOWN0 + 2 * KF):
                split_hi(n, n % SPLIT)
                if n == DOWN0 + 2 * LAG:
                    hidden_hi(FF_SLICES)

        @block.vector
        def _(dve):
            steps = [0]

            def then(*instructions):
                for ins in instructions:
                    steps[0] += 1
                    ins.then_inc(dve_step, 1)
                dve.wait_ge(dve_step, steps[0])

            def split_lo(n, slot):
                dve.wait_ge(hi_done, n + 1)
                dve.tensor_tensor(w_lo[:, slot, :], w_raw[:, slot, :], w_hi[:, slot, :].bitcast(F32),
                                  ALU.subtract).then_inc(lo_done, 1)

            counts = {"scaled": 0, "turned": 0}

            def turned_out(banks, w, hi, lo):
                counts["turned"] += 1
                dve.wait_ge(turned, counts["turned"])
                if counts["scaled"]:
                    dve.wait_ge(turn_lo, counts["scaled"])
                for t in range(TT):
                    weights = par[:, w:w + 4].unsqueeze(2).to_broadcast([P, 4, P])
                    dve.tensor_tensor(scaled[:, t, :].rearrange("p (k s) -> p k s", k=4),
                                      banks[t][:].rearrange("p (k s) -> p k s", k=4), weights,
                                      ALU.mult).then_inc(scaled_ready, 1)
                for t in range(TT):
                    counts["scaled"] += 1
                    dve.wait_ge(turn_hi, counts["scaled"])
                    tok = slice(P * t, P * (t + 1))
                    dve.tensor_tensor(lo[:, :, tok], scaled[:, t, :].rearrange("p (k s) -> p k s", k=4),
                                      hi[:, :, tok].bitcast(F32), ALU.subtract).then_inc(turn_lo, 1)

            def x_block(b):
                turned_out(aux[2 * (b % 2):2 * (b % 2) + 2], R_N1 + 4 * b,
                           act_hi[:, 4 * b:4 * b + 4, :], act_lo[:, 4 * b:4 * b + 4, :])

            def small_work(n):
                g, c = n // GC, n % GC
                if n in (1, 3, 5):
                    x_block((n + 1) // 2)
                if n == 6:
                    dve.wait_ge(x_squared, 8)
                    dve.tensor_reduce(tot, ss_x, AX.X, ALU.add).then_inc(x_tot, 1)
                    dve.wait_ge(x_root, 1)
                    then(dve.reciprocal(r1, root))
                    dve.scalar_tensor_tensor(out=r1sq, in0=r1, scalar=1.0 / DQK, in1=r1, op0=ALU.mult,
                                             op1=ALU.mult).then_inc(r1_ready, 1)
                if n == 7:
                    dve.wait_ge(wif_hi, 1)
                    dve.tensor_tensor(w_if_lo[:], w_if[:], w_if_hi[:].bitcast(F32), ALU.subtract)
                    dve.tensor_tensor(lam_prod, par[:, R_LAM:R_LAM + 2], par[:, R_LAM + 2:R_LAM + 4],
                                      ALU.mult).then_inc(wif_lo, 1)
                if 1 <= g <= 4 and c == LAG - 1:
                    for t in range(TT):
                        dve.wait_ge(squared, 2 * (g - 1) + t + 1)
                        then(dve.tensor_reduce(qk_ss[:, 4 * t:4 * t + 4],
                                               gated[:, t, :].rearrange("p (h d) -> p h d", h=4), AX.X, ALU.add))
                    dve.wait_ge(r1_ready, 1)
                    for t in range(TT):
                        v = dve.tensor_scalar(qk_v[:, 4 * t:4 * t + 4], qk_ss[:, 4 * t:4 * t + 4],
                                              r1sq[:, t:t + 1], None, ALU.mult)
                    v.then_inc(qk_var, 1)
                if 1 <= g <= 4 and c == LAG:
                    dve.wait_ge(qk_rooted, g)
                    then(dve.reciprocal(qk_f, qk_root))
                    then(*[dve.tensor_scalar(qk_f[:, 4 * t:4 * t + 4], qk_f[:, 4 * t:4 * t + 4],
                                             r1[:, t:t + 1], None, ALU.mult) for t in range(TT)])
                    banks = acc[2 * ((g - 1) % 2):2 * ((g - 1) % 2) + 2]
                    if g >= 2:
                        dve.wait_ge(qk_turned, g - 1)
                    for t in range(TT):
                        f = qk_f[:, 4 * t:4 * t + 4].unsqueeze(2).to_broadcast([P, 4, P])
                        dve.tensor_tensor(stage[:, t, :].rearrange("p (h d) -> p h d", h=4),
                                          banks[t][:].rearrange("p (h d) -> p h d", h=4), f,
                                          ALU.mult).then_inc(stage_ready, 1)
                if n == AT_GATES + LAG:
                    dve.wait_ge(gates_done, 1)
                    for t in range(TT):
                        s = dve.tensor_scalar(gate_cols[:, t, :], aux[2][:, 8 * t:8 * t + 8], r1[:, t:t + 1],
                                              None, ALU.mult)
                    s.then_inc(gates_read, 1)
                    dve.wait_ge(lam_exped, 1)
                    dve.scalar_tensor_tensor(out=neg_lam, in0=lam_exp[:, 1:2], scalar=-LAM_INIT,
                                             in1=lam_exp[:, 0:1], op0=ALU.add, op1=ALU.subtract
                                             ).then_inc(lam_read, 1)
                if n == AT_ROWS + LAG:
                    dve.wait_ge(rows_turned, 1)
                    dve.wait_ge(bias_landed, 32)
                    then(dve.tensor_scalar(f_pre[:], aux[3][0:HEADS, SEQ:2 * SEQ], bias_if[:, 1:2], None, ALU.add))
                    dve.scalar_tensor_tensor(out=f_abs[:], in0=f_pre[:], scalar=-1.0, in1=f_pre[:],
                                             op0=ALU.mult, op1=ALU.max).then_inc(f_ready, 1)
                    dve.wait_ge(ln_ready, 1)
                    then(dve.scalar_tensor_tensor(out=log_f[:], in0=f_pre[:], scalar=0.0, in1=f_ln[:],
                                                  op0=ALU.min, op1=ALU.subtract))
                    then(dve.tensor_tensor_scan(f_sum[:], log_f[:], zero_row[:], 0.0, ALU.add, ALU.add))
                    then(dve.scalar_tensor_tensor(out=a_row[:], in0=aux[3][0:HEADS, 0:SEQ],
                                                  scalar=bias_if[:, 0:1], in1=f_sum[:], op0=ALU.add,
                                                  op1=ALU.subtract))
                    then(dve.tensor_tensor_scan(m_run[:], a_row[:], a_row[:], NEG, ALU.max, ALU.max))
                    dve.tensor_scalar(neg_run[:], m_run[:], -1.0, None, ALU.mult)
                    dve.scalar_tensor_tensor(out=neg_m[:], in0=f_sum[:], scalar=-1.0, in1=m_run[:],
                                             op0=ALU.mult, op1=ALU.subtract).then_inc(rows_ready, 1)
                if n == AT_COLS + LAG:
                    dve.wait_ge(cols_turned, 1)
                    dve.tensor_copy(a_col, aux[2][:, 0:8]).then_inc(cols_read, 1)
                for h in range(HEADS):
                    if n == AT_SCORE[h] + LAG:
                        dve.wait_ge(scored, h + 1)
                        t0 = aux[1][:, 0:SEQ].rearrange("p (c k) -> p c k", c=2)
                        t1 = aux[0][:].rearrange("p (c k) -> p c k", c=2)
                        then(dve.tensor_tensor(t0[:, :, 64:P], t0[:, :, 64:P], chunk_mask[:], ALU.add),
                             dve.tensor_tensor(t1[:, :, 192:SEQ], t1[:, :, 192:SEQ], chunk_mask[:], ALU.add))
                        then(dve.tensor_reduce(a_max[:, 0:2], t0, AX.X, ALU.max),
                             dve.tensor_reduce(a_max[:, 2:4], t1, AX.X, ALU.max))
                        dve.tensor_scalar(a_nmax, a_max, -SCALE, None, ALU.mult).then_inc(maxed, 1)
                        dve.wait_ge(exped, h + 1)
                        then(dve.reciprocal(a_rec, a_sum))
                        then(*[dve.tensor_scalar(a_mix[:, t:t + 1], a_rec[:, 2 * t + 1:2 * t + 2], neg_lam,
                                                 None, ALU.mult) for t in range(TT)])
                        parts = (slice(0, P), slice(P, P + SEQ))
                        then(*[dve.tensor_scalar(a_tmp[:, parts[t]], probs[:, 1, parts[t]], a_mix[:, t:t + 1],
                                                 None, ALU.mult) for t in range(TT)])
                        if h:
                            dve.wait_ge(mat_turned, h)
                        for t in range(TT):
                            m = dve.scalar_tensor_tensor(out=a_mat[:, parts[t]], in0=probs[:, 0, parts[t]],
                                                         scalar=a_rec[:, 2 * t:2 * t + 1], in1=a_tmp[:, parts[t]],
                                                         op0=ALU.mult, op1=ALU.add)
                        m.then_inc(mat_ready, 1)
                    if n == AT_PV[h] + 2:
                        dve.wait_ge(y_squared, h + 1)
                        then(dve.reciprocal(y_rec, y_root))
                        then(dve.tensor_scalar(y_f, y_rec, 1.0 - LAM_INIT, None, ALU.mult))
                        dve.wait_ge(qk_turned, 4)
                        if h:
                            dve.wait_ge(y_turned, h)
                        if h == HEADS - 1:
                            dve.wait_ge(m_turned, 1)
                        for t in range(TT):
                            s = dve.tensor_scalar(stage[:, t, 0:DV], aux[3][:, DV * t:DV * (t + 1)],
                                                  y_f[:, t:t + 1], None, ALU.mult)
                        s.then_inc(y_scaled, 1)
                    if n == AT_Y[h] + LAG:
                        dve.wait_ge(y_turned, h + 1)
                        w = par[:, R_AN + 2 * h:R_AN + 2 * h + 2].unsqueeze(2).to_broadcast([P, 2, SEQ])
                        dve.tensor_tensor(scaled[:, 0, :].rearrange("p (k s) -> p k s", k=2),
                                          aux[2][:].rearrange("p (k s) -> p k s", k=2), w,
                                          ALU.mult).then_inc(y_mul, 1)
                        dve.wait_ge(y_hi_done, h + 1)
                        ks = slice(8 + 2 * h, 10 + 2 * h)
                        dve.tensor_tensor(y_lo[:, ks, :], scaled[:, 0, :].rearrange("p (k s) -> p k s", k=2),
                                          y_hi[:, ks, :].bitcast(F32), ALU.subtract).then_inc(y_lo_done, 1)
                if g in (G_MQ + 1, G_MK + 1) and c == 2 * LAG:
                    j = g - G_MQ - 1
                    for s in range(1, CONV_W):
                        taps = []
                        for b in range(HEADS):
                            if s == 1:
                                dve.wait_ge(conv_first, 4 * j + 2 * (b // 2) + 2)
                            w = R_CW + 8 * (CONV_W - 1 - s) + 4 * j + b
                            o = SEQ * (b % 2)
                            taps.append(dve.scalar_tensor_tensor(
                                out=conv[:, b, s:SEQ], in0=aux[b // 2][:, o:o + SEQ - s], scalar=par[:, w:w + 1],
                                in1=conv[:, b, s:SEQ], op0=ALU.mult, op1=ALU.add))
                        if s < CONV_W - 1:
                            then(*taps)
                    taps[-1].then_inc(conv_done, 1)
                for h in range(HEADS):
                    if n == AT_MS[h] + LAG:
                        dve.wait_ge(m_scored, h + 1)
                        dve.tensor_tensor(m_arg[:, 0:SEQ], aux[1][:, 0:SEQ], causal[:], ALU.add)
                        dve.tensor_tensor(m_arg[:, SEQ:SEQ + P], aux[1][:, P:SEQ], causal[:, 0:P],
                                          ALU.add).then_inc(m_masked, 1)
                        dve.wait_ge(m_exped, h + 1)
                        if h:
                            dve.wait_ge(mpv_done, h)
                        dve.scalar_tensor_tensor(out=m_w[:], in0=aux[0][:, 0:P + SEQ], scalar=SCALE, in1=m_exp[:],
                                                 op0=ALU.mult, op1=ALU.mult).then_inc(mw_ready, 1)
                    if n == AT_MPV[h] + LAG:
                        dve.wait_ge(mpv_done, h + 1)
                        for t in range(TT):
                            dve.tensor_copy(m_num[:, t, h, :], aux[2 + t][:, 0:DV + 1]).then_inc(mnum_read, 1)
                if n == AT_MPV[3] + LAG:
                    dve.wait_ge(mnum_read, 8)
                    dve.wait_ge(msq_done, 4)
                    den = m_num[:, :, :, DV:DV + 1].rearrange("p t h o -> p t (h o)")
                    den8 = m_den.rearrange("p (t h) -> p t h", t=TT)
                    then(dve.scalar_tensor_tensor(out=den8, in0=den, scalar=-1.0, in1=den, op0=ALU.mult,
                                                  op1=ALU.max))
                    then(dve.tensor_tensor(m_den, m_den, exp_nm, ALU.max))
                    then(dve.reciprocal(m_rec, m_den))
                    then(dve.tensor_tensor(m_v, m_ss, m_rec, ALU.mult))
                    dve.tensor_tensor(m_v2, m_v, m_rec, ALU.mult).then_inc(m_var, 1)
                    dve.wait_ge(m_rooted, 1)
                    then(dve.reciprocal(m_v, m_root))
                    then(dve.tensor_tensor(m_rec, m_rec, m_v, ALU.mult))
                if n in (AT_MY[0] - 1, AT_MY[1] - 1):
                    j = int(n > AT_MY[0])
                    if j:
                        dve.wait_ge(turned, 5)
                    else:
                        dve.wait_ge(m_turned, 2)
                    for t in range(TT):
                        dve.wait_ge(sig_done, 2 * j + t + 1)
                        for b in range(2):
                            h = 2 * j + b
                            s = dve.scalar_tensor_tensor(
                                out=stage[:, t, DV * b:DV * (b + 1)], in0=m_num[:, t, h, 0:DV],
                                scalar=m_rec[:, 4 * t + h:4 * t + h + 1], in1=gated[:, t, DV * b:DV * (b + 1)],
                                op0=ALU.mult, op1=ALU.mult)
                        s.then_inc(stage_ready, 1)
                if n in (AT_MY[0] + LAG, AT_MY[1] + LAG):
                    j = int(n > OUT0)
                    turned_out(aux[0:2], R_MN + 4 * j, y_hi[:, 4 * j:4 * j + 4, :], y_lo[:, 4 * j:4 * j + 4, :])

            def free_group(n):
                g, c = n // GC, n % GC
                if 1 <= g <= len(IN_COLS) and c == LAG + 1:
                    last = {G_AQ: (stage_ready, 2), G_AQ + 1: (stage_ready, 4), G_AK: (stage_ready, 6),
                            G_AK + 1: (stage_ready, 8), G_AV: (av_ready, 2), G_AV + 1: (av_ready, 4),
                            G_MQ: (stage_ready, 10), G_MK: (stage_ready, 12), G_MV: (mv_ready, 2),
                            G_MV + 1: (mv_ready, 4), G_MO: (sig_done, 2), G_MO + 1: (sig_done, 4)}[g - 1]
                    dve.wait_ge(*last)
                    dve.sem_inc(acc_free, 1)

            def x1_group(g):
                dve.wait_ge(chunk_used, OUT0 + (g + 1) * GC)
                for t in range(TT):
                    r = res[:, t, NG * g:NG * (g + 1)]
                    dve.tensor_tensor(r, r, acc[2 * (g % 2) + t][:], ALU.add).then_inc(x1_ready, 1)

            def x1_block(g):
                turned_out(aux[0:2], R_N2 + 4 * g, act_hi[:, 4 * g:4 * g + 4, :], act_lo[:, 4 * g:4 * g + 4, :])

            def hidden(i):
                dve.wait_ge(chunk_used, i * FF_CHUNKS + FF0)
                dve.wait_ge(gate_act, i * 2)
                if isinstance(i, int):
                    dve.wait_ge(hid_turned, i - 1)
                for t in range(TT):
                    dve.scalar_tensor_tensor(out=stage[:, t, :], in0=acc[2 + t][:], scalar=r2[:, t:t + 1],
                                             in1=gated[:, t, :], op0=ALU.mult, op1=ALU.mult).then_inc(hid_ready, 1)

            def hidden_lo(i):
                for t in range(TT):
                    dve.wait_ge(hid_hi_done, i * 2 + (t - 1))
                    ks, tok = bass.ds(i * 4 - 4, 4), slice(P * t, P * (t + 1))
                    dve.tensor_tensor(hid_lo[:, ks, tok], aux[t][:].rearrange("p (k s) -> p k s", k=4),
                                      hid_hi[:, ks, tok].bitcast(F32), ALU.subtract).then_inc(hid_lo_done, 1)

            dve.wait_ge(par_ready, 1)
            x_block(0)
            for n in range(FF0):
                split_lo(n, n % SPLIT)
                small_work(n)
                free_group(n)
                if n > OUT0 + GC and (n - OUT0) % GC == LAG - 1:
                    x1_group((n - OUT0) // GC - 1)
                if n > OUT0 + GC and (n - OUT0) % GC == 2 * LAG:
                    x1_block((n - OUT0) // GC - 1)

            def ff_slice(i, first):
                for c in range(FF_CHUNKS):
                    split_lo(i * FF_CHUNKS + (FF0 + c), c % SPLIT)
                    if first and c == LAG - 1:
                        x1_group(3)
                    if first and c == 2 * LAG:
                        x1_block(3)
                        dve.wait_ge(x1_squared, 4)
                        dve.tensor_reduce(tot, ss_x1, AX.X, ALU.add).then_inc(x1_tot, 1)
                        dve.wait_ge(x1_root, 1)
                        dve.reciprocal(r2, root).then_inc(r2_ready, 1)
                        dve.wait_ge(r2_ready, 1)
                    if not first and c == LAG - 1:
                        hidden(i)
                    if not first and c == 2 * LAG:
                        hidden_lo(i)

            ff_slice(0, True)
            with dve.Fori(1, FF_SLICES) as i:
                ff_slice(i, False)

            def output(p):
                banks = [[acc[0], acc[1], aux[2], aux[3]], [acc[2], acc[3], aux[0], aux[1]]][p]
                for j in range(4):
                    if p:
                        dve.wait_ge(bank_done, j + 1)
                    else:
                        dve.wait_ge(chunk_used, DOWN0 + KF)
                    col, t = CH * p + NG * (j // 2), j % 2
                    r = res[:, t, col:col + NG]
                    dve.tensor_tensor(r, r, banks[j][:], ALU.add).then_inc(out_ready, 1)

            for n in range(DOWN0, DOWN0 + 2 * KF):
                split_lo(n, n % SPLIT)
                if n == DOWN0 + LAG - 1:
                    hidden(FF_SLICES)
                if n == DOWN0 + 2 * LAG:
                    hidden_lo(FF_SLICES)
                if n == DOWN0 + KF + LAG - 1:
                    output(0)
            output(1)


_INS = ['x', 'norm1_w', 'w_in', 'conv_w', 'conv_b', 'i_bias', 'f_bias', 'm_norm_w', 'q_norm_w', 'k_norm_w',
        'lambda_q1', 'lambda_k1', 'lambda_q2', 'lambda_k2', 'a_norm_w', 'w_out', 'norm2_w', 'w_gate',
        'w_up', 'w_down']


def kernel(**inputs):
    import concourse.bacc as bacc
    from concourse.bass_utils import run_bass_kernel_spmd

    nc = bacc.Bacc("TRN2", target_bir_lowering=False, num_devices=1)
    arrays, args = {}, []
    for name in _INS:
        a = np.ascontiguousarray(inputs[name])
        arrays[f"in_{name}"] = a
        args.append(nc.dram_tensor(f"in_{name}", a.shape, mybir.dt.from_np(a.dtype), kind="ExternalInput").ap())
    args.append(nc.dram_tensor("out_0", (1, SEQ, D), F32, kind="ExternalOutput").ap())
    hybrid_block_kernel(nc, *args)
    r = run_bass_kernel_spmd(nc, [arrays], core_ids=[0])
    return r.results[0]["out_0"]
```

```python
import math
from contextlib import ExitStack

import numpy as np

import concourse.bass as bass
from concourse import mybir

F32 = mybir.dt.float32
F32R = mybir.dt.float32r
ALU = mybir.AluOpType
ACT = mybir.ActivationFunctionType
AX = mybir.AxisListType

P = 128
SEQ = 256
TT = SEQ // P
D = 2048
KT = D // P
D_FF = 5632
KF = D_FF // P
NG = 512
CH = 2 * NG
HEADS = 4
DQK = 128
DV = 256
CONV_W = 4
EPS = 1e-6
NEG = -1e30
LAM_INIT = 0.8 - 0.6 * math.exp(-0.3 * 0)
SCALE = DQK ** -0.5
RAW = 4
SPLIT = 4

C_MQK, C_MV, C_MO, C_IF = 0, 1024, 2048, 3072
C_AQ, C_AK, C_AV = 3080, 4104, 5128
G_AQ, G_AK, G_AV, G_MQ, G_MK, G_MV, G_MO = 0, 2, 4, 6, 7, 8, 10
IN_COLS = [C_AQ + NG * g for g in range(6)] + [NG * g for g in range(6)]
GC = KT // 2
IN_CHUNKS = len(IN_COLS) * GC
OUT0 = IN_CHUNKS
OUT_GROUPS = D // NG
FF0 = OUT0 + OUT_GROUPS * GC
FF_SLICES = D_FF // NG
FF_CHUNKS = 2 * GC
DOWN0 = FF0 + FF_SLICES * FF_CHUNKS

R_N1, R_N2, R_MN, R_AN, R_CW, R_CB, R_QN, R_KN, R_LAM = 0, 16, 32, 40, 48, 80, 88, 89, 90
N_PAR = 94

AT_PAR, AT_GATES, AT_ROWS, AT_COLS = 5, 14, 18, 28
AT_SCORE = [39 + 5 * h for h in range(HEADS)]
AT_PT = [p + 4 for p in AT_SCORE]
AT_PV = [p + 5 for p in AT_SCORE]
AT_Y = [p + 7 for p in AT_SCORE]
AT_CONV = [GC * (G_MQ + 1) + 7, GC * (G_MK + 1) + 7]
AT_MS = [73 + 4 * h for h in range(HEADS)]
AT_MPV = [p + 4 for p in AT_MS]
AT_MY = [94, 99]
LAG = 3


def hybrid_block_kernel(nc, x, norm1_w, w_in, conv_w, conv_b, i_bias, f_bias, m_norm_w, q_norm_w,
                        k_norm_w, lambda_q1, lambda_k1, lambda_q2, lambda_k2, a_norm_w, w_out,
                        norm2_w, w_gate, w_up, w_down, out):
    ctx = ExitStack()
    with ctx:
        def sb(name, shape, dt=F32, stack=ctx, parts=P):
            return stack.enter_context(nc.sbuf_tensor(name, [parts] + shape, dt))

        def sem(name):
            return ctx.enter_context(nc.semaphore(name))

        res = sb("res", [TT, D])
        act_hi = sb("act_hi", [KT, SEQ], F32R)
        act_lo = sb("act_lo", [KT, SEQ], F32R)
        w_raw = sb("w_raw", [RAW, CH])
        w_hi = sb("w_hi", [SPLIT, CH], F32R)
        w_lo = sb("w_lo", [SPLIT, CH], F32R)
        stage = sb("stage", [TT, NG])
        scaled = sb("scaled", [TT, NG])
        gated = sb("gated", [TT, NG])
        ident = sb("ident", [P])
        par = sb("par", [N_PAR])
        small = sb("small", [168])
        ss_x = small[:, 0:8].rearrange("p (t b) -> p t b", t=TT)
        ss_x1 = small[:, 8:16].rearrange("p (t b) -> p t b", t=TT)
        tot = small[:, 16:18]
        root = small[:, 18:20]
        r1 = small[:, 20:22]
        r1sq = small[:, 22:24]
        r2 = small[:, 24:26]
        qk_ss = small[:, 26:34]
        qk_v = small[:, 34:42]
        qk_root = small[:, 42:50]
        qk_f = small[:, 50:58]
        qk_n = small[:, 160:168]
        eps = small[:, 58:59]
        lam_prod = small[:, 59:61]
        lam_exp = small[:, 61:63]
        neg_lam = small[:, 63:64]
        a_max = small[:, 64:68]
        a_nmax = small[:, 68:72]
        a_sum = small[:, 72:76]
        a_rec = small[:, 76:80]
        a_mix = small[:, 80:82]
        y_ss = small[:, 82:84]
        y_root = small[:, 84:86]
        y_rec = small[:, 86:88]
        y_f = small[:, 88:90]
        a_col = small[:, 90:98]
        exp_nm = small[:, 98:106]
        m_ss = small[:, 106:114]
        m_den = small[:, 114:122]
        m_rec = small[:, 122:130]
        m_v = small[:, 130:138]
        m_v2 = small[:, 138:146]
        m_root = small[:, 146:154]
        one_col = small[:, 154:155]

        mix = ExitStack()
        y_hi = sb("y_hi", [KT, SEQ], F32R, mix)
        y_lo = sb("y_lo", [KT, SEQ], F32R, mix)
        mv = sb("mv", [TT, HEADS, DV + 1], F32, mix)
        probs = sb("probs", [2, P + SEQ], F32, mix)
        a_tmp = sb("a_tmp", [P + SEQ], F32, mix)
        a_mat = sb("a_mat", [P + SEQ], F32, mix)
        a_turn = sb("a_turn", [P + SEQ], F32, mix)
        m_arg = sb("m_arg", [P + SEQ], F32, mix)
        m_exp = sb("m_exp", [P + SEQ], F32, mix)
        m_w = sb("m_w", [P + SEQ], F32, mix)
        causal = sb("causal", [SEQ], F32, mix)
        chunk_mask = sb("chunk_mask", [2, 64], F32, mix)
        ones = sb("ones", [P], F32, mix)
        par_rows = sb("par_rows", [P], F32, mix, R_N2)
        par_rows2 = sb("par_rows2", [P], F32, mix, N_PAR - R_N2)
        w_if = sb("w_if", [KT, 8], F32, mix)
        w_if_parts = sb("w_if_parts", [KT, 16], F32R, mix)
        gate_part = sb("gate_part", [TT, 8], F32, mix)
        gate_cols = sb("gate_cols", [TT, 8], F32, mix)
        select = sb("select", [HEADS, P], F32, mix, HEADS)
        bias_if = sb("bias_if", [2], F32, mix, HEADS)
        zero_row = sb("zero_row", [SEQ], F32, mix, HEADS)
        f_pre = sb("f_pre", [SEQ], F32, mix, HEADS)
        f_abs = sb("f_abs", [SEQ], F32, mix, HEADS)
        f_exp = sb("f_exp", [SEQ], F32, mix, HEADS)
        f_ln = sb("f_ln", [SEQ], F32, mix, HEADS)
        log_f = sb("log_f", [SEQ], F32, mix, HEADS)
        f_sum = sb("f_sum", [SEQ], F32, mix, HEADS)
        a_row = sb("a_row", [SEQ], F32, mix, HEADS)
        m_run = sb("m_run", [SEQ], F32, mix, HEADS)
        neg_run = sb("neg_run", [SEQ], F32, mix, HEADS)
        neg_m = sb("neg_m", [SEQ], F32, mix, HEADS)
        attn = ExitStack()
        aq = sb("aq", [2 * HEADS, SEQ], F32, attn)
        ak = sb("ak", [2 * HEADS, SEQ], F32, attn)
        av = sb("av", [TT, HEADS * DV], F32, attn)
        attn.close()
        lstm = ExitStack()
        conv = sb("conv", [HEADS, SEQ], F32, lstm)
        mq = sb("mq", [HEADS, SEQ], F32, lstm)
        mk = sb("mk", [HEADS, SEQ], F32, lstm)
        m_num = sb("m_num", [TT, HEADS, DV + 1], F32, lstm)
        lstm.close()
        mix.close()
        ff = ExitStack()
        hid_hi = sb("hid_hi", [KF, SEQ], F32R, ff)
        hid_lo = sb("hid_lo", [KF, SEQ], F32R, ff)
        ff.close()

        acc = [ctx.enter_context(nc.psum_tensor(f"acc{i}", [P, NG], F32)) for i in range(4)]
        aux = [ctx.enter_context(nc.psum_tensor(f"aux{i}", [P, NG], F32)) for i in range(4)]

        raw_landed = [sem(f"raw_landed{s}") for s in range(RAW)]
        hi_done = sem("hi_done")
        lo_done = sem("lo_done")
        chunk_used = sem("chunk_used")
        acc_free = sem("acc_free")
        x_landed = [sem(f"x_landed{b}") for b in range(4)]
        par_landed = sem("par_landed")
        par2_landed = sem("par2_landed")
        wif_landed = sem("wif_landed")
        bias_landed = sem("bias_landed")
        zeroed = sem("zeroed")
        const_ready = sem("const_ready")
        ident_ready = sem("ident_ready")
        par_turned = sem("par_turned")
        par_ready = sem("par_ready")
        turned = sem("turned")
        scaled_ready = sem("scaled_ready")
        turn_hi = sem("turn_hi")
        turn_lo = sem("turn_lo")
        x_squared = sem("x_squared")
        x_tot = sem("x_tot")
        x_root = sem("x_root")
        r1_ready = sem("r1_ready")
        wif_hi = sem("wif_hi")
        wif_lo = sem("wif_lo")
        squared = sem("squared")
        qk_var = sem("qk_var")
        qk_rooted = sem("qk_rooted")
        stage_ready = sem("stage_ready")
        qk_turned = sem("qk_turned")
        qk_out = sem("qk_out")
        av_ready = sem("av_ready")
        gates_done = sem("gates_done")
        gates_read = sem("gates_read")
        lam_exped = sem("lam_exped")
        lam_read = sem("lam_read")
        rows_turned = sem("rows_turned")
        f_ready = sem("f_ready")
        ln_ready = sem("ln_ready")
        rows_ready = sem("rows_ready")
        cols_turned = sem("cols_turned")
        cols_read = sem("cols_read")
        scored = sem("scored")
        maxed = sem("maxed")
        exped = sem("exped")
        mat_ready = sem("mat_ready")
        mat_turned = sem("mat_turned")
        mat_out = sem("mat_out")
        pv_done = sem("pv_done")
        y_squared = sem("y_squared")
        y_factor = sem("y_factor")
        y_scaled = sem("y_scaled")
        y_turned = sem("y_turned")
        y_mul = sem("y_mul")
        y_hi_done = sem("y_hi_done")
        y_lo_done = sem("y_lo_done")
        m_turned = sem("m_turned")
        conv_first = sem("conv_first")
        conv_done = sem("conv_done")
        silu_done = sem("silu_done")
        mv_ready = sem("mv_ready")
        m_scored = sem("m_scored")
        m_masked = sem("m_masked")
        m_exped = sem("m_exped")
        mw_ready = sem("mw_ready")
        mpv_done = sem("mpv_done")
        mnum_read = sem("mnum_read")
        msq_done = sem("msq_done")
        m_var = sem("m_var")
        m_rooted = sem("m_rooted")
        sig_done = sem("sig_done")
        x1_ready = sem("x1_ready")
        x1_squared = sem("x1_squared")
        x1_tot = sem("x1_tot")
        x1_root = sem("x1_root")
        r2_ready = sem("r2_ready")
        gate_act = sem("gate_act")
        hid_ready = sem("hid_ready")
        hid_turned = sem("hid_turned")
        hid_hi_done = sem("hid_hi_done")
        hid_lo_done = sem("hid_lo_done")
        bank_done = sem("bank_done")
        out_ready = sem("out_ready")
        out_stored = sem("out_stored")
        act_step = sem("act_step")
        dve_step = sem("dve_step")

        def tiles(w):
            return w[0].rearrange("(k p) n -> p k n", p=P)

        win_t, wout_t, wgate_t, wup_t, wdown_t = (tiles(w) for w in (w_in, w_out, w_gate, w_up, w_down))
        x_t = x[0].rearrange("(t p) n -> p t n", p=P)
        out_t = out[0].rearrange("(t p) n -> p t n", p=P)

        block = ctx.enter_context(nc.Block())

        @block.sync
        def _(sp):
            def load(n, src, slot, wait=True):
                if wait:
                    sp.wait_ge(lo_done, n - (RAW - 1))
                dst = w_raw[:, slot, :].rearrange("p (k n) -> p k n", k=src.shape[1])
                sp.dma_start(dst, src).then_inc(raw_landed[slot], 16)

            for g, col in enumerate(IN_COLS):
                for c in range(GC):
                    if g == 0 and c < 4:
                        sp.dma_start(res[:, :, NG * c:NG * (c + 1)],
                                     x_t[:, :, NG * c:NG * (c + 1)]).then_inc(x_landed[c], 16)
                    load(g * GC + c, win_t[:, 2 * c:2 * c + 2, col:col + NG], c % RAW, g * GC + c >= RAW)
            with sp.Fori(1, OUT_GROUPS + 1) as g:
                for c in range(GC):
                    k = (2 * c + KT // 2) % KT
                    load(g * GC + (OUT0 - GC + c), wout_t[:, k:k + 2, bass.ds(g * NG - NG, NG)], c % RAW)
            with sp.Fori(1, FF_SLICES + 1) as i:
                for c in range(FF_CHUNKS):
                    w = wgate_t if c < GC else wup_t
                    k = 2 * (c % GC)
                    load(i * FF_CHUNKS + (FF0 - FF_CHUNKS + c), w[:, k:k + 2, bass.ds(i * NG - NG, NG)], c % RAW)
            for p in range(2):
                with sp.Fori(1, KF // RAW + 1) as i:
                    for k in range(RAW):
                        load(i * RAW + (DOWN0 + p * KF - RAW + k),
                             wdown_t[:, bass.ds(i * RAW + (k - RAW), 1), CH * p:CH * (p + 1)], k)
            for j in range(8):
                col, t = NG * (j // 2), j % 2
                sp.wait_ge(out_ready, j + 1)
                sp.dma_start(out_t[:, t, col:col + NG], res[:, t, col:col + NG]).then_inc(out_stored, 16)
            sp.wait_ge(out_stored, 16 * 8)

        @block.gpsimd
        def _(pool):
            pool.memset(ident[:], 0.0).then_inc(zeroed, 1)
            pool.wait_ge(zeroed, 1)
            pool.affine_select(out=ident[:], in_=ident[:], compare_op=ALU.not_equal, fill=1.0, base=0,
                               pattern=[[-1, P]], channel_multiplier=1).then_inc(ident_ready, 1)
            pool.memset(causal[:], 0.0).then_inc(zeroed, 1)
            pool.memset(chunk_mask[:], 0.0).then_inc(zeroed, 1)
            pool.memset(select[:], 0.0).then_inc(zeroed, 1)
            pool.memset(ones[:], 1.0).then_inc(const_ready, 1)
            pool.memset(zero_row[:], 0.0).then_inc(const_ready, 1)
            pool.memset(mv[:, :, :, DV:DV + 1], 1.0).then_inc(const_ready, 1)
            pool.memset(eps, EPS).then_inc(const_ready, 1)
            pool.memset(one_col, 1.0).then_inc(const_ready, 1)
            pool.wait_ge(zeroed, 4)
            pool.affine_select(out=causal[:, 0:P], in_=causal[:, 0:P], compare_op=ALU.is_ge, fill=NEG,
                               base=0, pattern=[[1, P]], channel_multiplier=-1).then_inc(const_ready, 1)
            pool.affine_select(out=chunk_mask[:], in_=chunk_mask[:], compare_op=ALU.is_ge, fill=NEG,
                               base=-64, pattern=[[0, 2], [0, 64]], channel_multiplier=1).then_inc(const_ready, 1)
            pool.affine_select(out=select[:], in_=select[:], compare_op=ALU.not_equal, fill=1.0, base=0,
                               pattern=[[-1, HEADS], [0, P]], channel_multiplier=1).then_inc(const_ready, 1)

            rows = [(norm2_w[0], R_N2), (m_norm_w[0].rearrange("h d -> (h d)"), R_MN),
                    (a_norm_w[0].rearrange("h d -> (h d)"), R_AN),
                    (conv_w[0].rearrange("j c -> (j c)"), R_CW), (conv_b[0], R_CB),
                    (q_norm_w[0], R_QN), (k_norm_w[0], R_KN), (lambda_q1[0], R_LAM),
                    (lambda_q2[0], R_LAM + 1), (lambda_k1[0], R_LAM + 2), (lambda_k2[0], R_LAM + 3)]
            for src, r in rows:
                n = src.shape[0] // P
                pool.dma_start(par_rows2[r - R_N2:r - R_N2 + n, :],
                               src.rearrange("(r c) -> r c", c=P)).then_inc(par2_landed, 16)
            pool.dma_start(w_if[:], win_t[:, :, C_IF:C_IF + 8]).then_inc(wif_landed, 16)
            pool.dma_start(bias_if[:, 0:1], i_bias[0].rearrange("(h o) -> h o", o=1)).then_inc(bias_landed, 16)
            pool.dma_start(bias_if[:, 1:2], f_bias[0].rearrange("(h o) -> h o", o=1)).then_inc(bias_landed, 16)

        CONSTS = 8

        parts = (slice(0, P), slice(P, P + SEQ))

        @block.tensor
        def _(pe):
            def chunk(n, slot, banks, kts, width, hi, lo, first, last, by_bank=False):
                pe.wait_ge(lo_done, n + 1)
                for j in range(width):
                    for kk, k in enumerate(kts):
                        cols = slice(NG * (kk * width + j), NG * (kk * width + j + 1))
                        for t in range(TT):
                            tok = slice(P * t, P * (t + 1))
                            bank = banks[t][j]
                            pe.matmul(bank[:], hi[:, k, tok], w_lo[:, slot, cols],
                                      start=first and kk == 0, stop=False)
                            pe.matmul(bank[:], lo[:, k, tok], w_hi[:, slot, cols], start=False, stop=False)
                            mm = pe.matmul(bank[:], hi[:, k, tok], w_hi[:, slot, cols], start=False,
                                           stop=last and kk == len(kts) - 1)
                            if by_bank:
                                mm.then_inc(bank_done, 1)
                if not by_bank:
                    mm.then_inc(chunk_used, 1)

            def turn(src, banks, done):
                for t in range(TT):
                    for b in range(4):
                        mm = pe.transpose(banks[t][:, P * b:P * (b + 1)], src[:, t, P * b:P * (b + 1)], ident[:])
                    mm.then_inc(done, 1)

            def turn_x(b):
                pe.wait_ge(x_landed[b], 16)
                if b >= 2:
                    pe.wait_ge(turn_lo, 2 * (b - 1))
                turn(res[:, :, NG * b:NG * (b + 1)], aux[2 * (b % 2):2 * (b % 2) + 2], turned)

            def gates():
                pe.wait_ge(wif_lo, 1)
                pe.wait_ge(const_ready, CONSTS)
                pe.wait_ge(turn_lo, 8)
                for t in range(TT):
                    o = aux[2][:, 16 * t:16 * t + 16]
                    for k in range(KT):
                        a, b = act_hi[:, k, P * t:P * (t + 1)], act_lo[:, k, P * t:P * (t + 1)]
                        pe.matmul(o, a, w_if_parts[:, k, :], start=(k == 0), stop=False)
                        pe.matmul(o[:, 0:8], b, w_if_parts[:, k, 0:8], start=False, stop=(k == KT - 1))
                pe.matmul(aux[2][:, 32:34], ones[:], lam_prod, start=True, stop=True).then_inc(gates_done, 1)

            def gate_rows():
                pe.wait_ge(gates_read, 1)
                for j in range(2):
                    for t in range(TT):
                        mm = pe.transpose(aux[3][0:HEADS, SEQ * j + P * t:SEQ * j + P * (t + 1)],
                                          gate_cols[:, t, HEADS * j:HEADS * (j + 1)], ident[:])
                mm.then_inc(rows_turned, 1)

            def gate_columns():
                pe.wait_ge(rows_ready, 1)
                pe.wait_ge(lam_read, 1)
                for j, row in enumerate((a_row, neg_m)):
                    for t in range(TT):
                        o = 8 * j + 4 * t
                        mm = pe.transpose(aux[2][:, o:o + 4], row[:, P * t:P * (t + 1)], ident[0:4, 0:4])
                mm.then_inc(cols_turned, 1)

            def scores(h):
                if h == 0:
                    pe.wait_ge(qk_out, 8)
                else:
                    pe.wait_ge(exped, h)
                for c in range(2):
                    b = 2 * h + c
                    pe.matmul(aux[1][:, P * c:P * (c + 1)], aq[:, b, 0:P], ak[:, b, 0:P], start=True, stop=True)
                    mm = pe.matmul(aux[0][:, SEQ * c:SEQ * (c + 1)], aq[:, b, P:SEQ], ak[:, b, :],
                                   start=True, stop=True)
                mm.then_inc(scored, 1)

            def turn_mat(h):
                pe.wait_ge(mat_ready, h + 1)
                if h:
                    pe.wait_ge(mat_out, h)
                for b in range(3):
                    mm = pe.transpose(aux[2][:, P * b:P * (b + 1)], a_mat[:, P * b:P * (b + 1)], ident[:])
                mm.then_inc(mat_turned, 1)

            def attend(h):
                pe.wait_ge(mat_out, h + 1)
                pe.wait_ge(av_ready, 2 * (h // 2 + 1))
                if h:
                    pe.wait_ge(y_mul, h)
                v = slice(DV * h, DV * (h + 1))
                pe.matmul(aux[3][:, 0:DV], a_turn[:, 0:P], av[:, 0, v], start=True, stop=True)
                pe.matmul(aux[3][:, DV:2 * DV], a_turn[:, P:2 * P], av[:, 0, v], start=True, stop=False)
                pe.matmul(aux[3][:, DV:2 * DV], a_turn[:, 2 * P:3 * P], av[:, 1, v],
                          start=False, stop=True).then_inc(pv_done, 1)

            def turn_y(h):
                pe.wait_ge(y_scaled, h + 1)
                for b in range(2):
                    for t in range(TT):
                        mm = pe.transpose(aux[3][:, SEQ * b + P * t:SEQ * b + P * (t + 1)],
                                          stage[:, t, P * b:P * (b + 1)], ident[:])
                mm.then_inc(y_turned, 1)

            def turn_mqk(j):
                pe.wait_ge(stage_ready, 10 + 2 * j)
                if j == 0:
                    pe.wait_ge(exped, HEADS)
                else:
                    pe.wait_ge(conv_done, j)
                for b in range(HEADS):
                    for t in range(TT):
                        o = SEQ * (b % 2) + P * t
                        mm = pe.transpose(aux[b // 2][:, o:o + P], stage[:, t, P * b:P * (b + 1)], ident[:])
                mm.then_inc(m_turned, 1)

            def lstm_scores(h):
                if h == 0:
                    pe.wait_ge(silu_done, 2)
                else:
                    pe.wait_ge(mw_ready, h)
                pe.matmul(aux[0][:, 0:SEQ], mk[:, h, 0:P], mq[:, h, :], start=True, stop=True)
                pe.matmul(aux[0][:, SEQ:SEQ + P], mk[:, h, P:SEQ], mq[:, h, P:SEQ], start=True, stop=True)
                pe.matmul(aux[1][:, 0:SEQ], select[:, h, :], neg_run[:], start=True,
                          stop=True).then_inc(m_scored, 1)

            def lstm_attend(h):
                pe.wait_ge(mw_ready, h + 1)
                pe.wait_ge(mv_ready, 2 * (h // 2 + 1))
                if h == 0:
                    pe.wait_ge(y_mul, HEADS)
                else:
                    pe.wait_ge(mnum_read, 2 * h)
                    pe.wait_ge(msq_done, h)
                pe.matmul(aux[2][:, 0:DV + 1], m_w[:, 0:P], mv[:, 0, h, :], start=True, stop=True)
                pe.matmul(aux[3][:, 0:DV + 1], m_w[:, P:2 * P], mv[:, 0, h, :], start=True, stop=False)
                pe.matmul(aux[3][:, 0:DV + 1], m_w[:, 2 * P:3 * P], mv[:, 1, h, :], start=False,
                          stop=True).then_inc(mpv_done, 1)

            pe.wait_ge(ident_ready, 1)
            pe.wait_ge(par_landed, 16)
            pe.transpose(acc[3][:, 0:R_N2], par_rows[:], ident[0:R_N2, 0:R_N2]).then_inc(par_turned, 1)
            turn_x(0)
            turn_x(1)

            for n in range(IN_CHUNKS):
                g, c = n // GC, n % GC
                if c == 0 and g >= 2:
                    pe.wait_ge(acc_free, g - 1)
                if g == 0 and c % 2 == 0:
                    pe.wait_ge(turn_lo, c + 2)
                banks = acc[2 * (g % 2):2 * (g % 2) + 2]
                chunk(n, n % SPLIT, [[b] for b in banks], (2 * c, 2 * c + 1), 1, act_hi, act_lo,
                      c == 0, c == GC - 1)
                if n in (0, 2):
                    turn_x(2 + n // 2)
                if n == AT_PAR:
                    pe.wait_ge(par2_landed, 16 * 11)
                    pe.wait_ge(turn_lo, 6)
                    pe.transpose(aux[0][:, 0:N_PAR - R_N2], par_rows2[:],
                                 ident[0:N_PAR - R_N2, 0:N_PAR - R_N2]).then_inc(par_turned, 1)
                if n == AT_GATES:
                    gates()
                if n == AT_ROWS:
                    gate_rows()
                if n == AT_COLS:
                    gate_columns()
                if 1 <= g <= 4 and c == LAG:
                    pe.wait_ge(stage_ready, 2 * g)
                    if g >= 2:
                        pe.wait_ge(qk_out, 2 * (g - 1))
                    else:
                        pe.wait_ge(par_ready, 2)
                    turn(stage, aux[0:2], qk_turned)
                for h in range(HEADS):
                    if n == AT_SCORE[h]:
                        scores(h)
                    if n == AT_PT[h]:
                        turn_mat(h)
                    if n == AT_PV[h]:
                        attend(h)
                    if n == AT_Y[h]:
                        turn_y(h)
                    if n == AT_MS[h]:
                        lstm_scores(h)
                    if n == AT_MPV[h]:
                        lstm_attend(h)
                if g in (G_MQ + 1, G_MK + 1) and c == LAG:
                    turn_mqk(g - G_MQ - 1)
                if n == AT_MY[0]:
                    pe.wait_ge(stage_ready, 14)
                    turn(stage, aux[0:2], turned)

            for n in range(OUT0, FF0):
                g, c = divmod(n - OUT0, GC)
                if c == 0:
                    if g < 2:
                        pe.wait_ge(acc_free, len(IN_COLS) - 1 + g)
                    else:
                        pe.wait_ge(x1_ready, 2 * (g - 1))
                if g == 0 and c == 4:
                    pe.wait_ge(turn_lo, 10)
                if g == 0 and c == 6:
                    pe.wait_ge(turn_lo, 12)
                k = (2 * c + KT // 2) % KT
                banks = acc[2 * (g % 2):2 * (g % 2) + 2]
                chunk(n, n % SPLIT, [[b] for b in banks], (k, k + 1), 1, y_hi, y_lo, c == 0, c == GC - 1)
                if n == AT_MY[1]:
                    pe.wait_ge(stage_ready, 16)
                    pe.wait_ge(turn_lo, 10)
                    turn(stage, aux[0:2], turned)
                if g >= 1 and c == LAG:
                    pe.wait_ge(x1_ready, 2 * g)
                    pe.wait_ge(turn_lo, 10 + 2 * g)
                    turn(res[:, :, NG * (g - 1):NG * g], aux[0:2], turned)

            def ff_slice(i, first):
                n = i * FF_CHUNKS + FF0
                for c in range(FF_CHUNKS):
                    if c == 0 and not first:
                        pe.wait_ge(gate_act, i * 2)
                    if c == 0 and first:
                        pe.wait_ge(x1_ready, 6)
                    if c == GC and not first:
                        pe.wait_ge(hid_ready, i * 2)
                    if c == GC and first:
                        pe.wait_ge(x1_ready, 8)
                    if first and c in (0, 2, 4, 6):
                        pe.wait_ge(turn_lo, 14 + c)
                    banks = acc[0:2] if c < GC else acc[2:4]
                    k = 2 * (c % GC)
                    chunk(n + c, c % SPLIT, [[b] for b in banks], (k, k + 1), 1, act_hi, act_lo,
                          c % GC == 0, c % GC == GC - 1)
                    if c == LAG and first:
                        pe.wait_ge(x1_ready, 8)
                        pe.wait_ge(turn_lo, 18)
                        turn(res[:, :, NG * 3:NG * 4], aux[0:2], turned)
                    if c == LAG and not first:
                        turn_hidden(i)

            def turn_hidden(i):
                pe.wait_ge(hid_ready, i * 2)
                pe.wait_ge(hid_lo_done, i * 2 - 2)
                turn(stage, aux[0:2], hid_turned)

            ff_slice(0, True)
            pe.wait_ge(turn_lo, 20)
            with pe.Fori(1, FF_SLICES) as i:
                ff_slice(i, False)

            for p in range(2):
                banks = [[[acc[0], aux[2]], [acc[1], aux[3]]], [[acc[2], aux[0]], [acc[3], aux[1]]]][p]
                for k in range(KF):
                    if p == 0 and k == 0:
                        pe.wait_ge(gate_act, 2 * FF_SLICES)
                    if p == 0 and k < KF - 4 and k % 4 == 0:
                        pe.wait_ge(hid_lo_done, 2 * (k // 4 + 1))
                    if p == 0 and k == KF - 4:
                        pe.wait_ge(hid_lo_done, 2 * FF_SLICES)
                    chunk(DOWN0 + p * KF + k, k % SPLIT, banks, (k,), 2, hid_hi, hid_lo,
                          k == 0, k == KF - 1, p == 1 and k == KF - 1)
                    if p == 0 and k == LAG:
                        turn_hidden(FF_SLICES)

        @block.scalar
        def _(act):
            steps = [0]

            def then(ins):
                steps[0] += 1
                ins.then_inc(act_step, 1)
                act.wait_ge(act_step, steps[0])

            def split_hi(n, slot):
                act.wait_ge(raw_landed[slot], 16 * (n // RAW + 1))
                if n >= SPLIT:
                    act.wait_ge(chunk_used, n - (SPLIT - 1))
                act.activation(w_hi[:, slot, :], w_raw[:, slot, :], ACT.Copy).then_inc(hi_done, 1)

            def split_hi_from(start, ahead, c):
                act.wait_ge(raw_landed[c % RAW], ahead * (16 // RAW) + 16 * ((start + c) // RAW + 1))
                act.wait_ge(chunk_used, ahead + (start + c - (SPLIT - 1)))
                act.activation(w_hi[:, c % SPLIT, :], w_raw[:, c % RAW, :], ACT.Copy).then_inc(hi_done, 1)

            def turned_hi(dst, j, t):
                act.wait_ge(scaled_ready, j)
                act.activation(dst, scaled[:, t, :].rearrange("p (k s) -> p k s", k=4),
                               ACT.Copy).then_inc(turn_hi, 1)

            act.dma_start(par_rows[R_N1:R_N1 + KT, :], norm1_w[0].rearrange("(r c) -> r c", c=P)).then_inc(par_landed, 16)

            def x_hi(b):
                for t in range(TT):
                    turned_hi(act_hi[:, 4 * b:4 * b + 4, P * t:P * (t + 1)], 2 * b + t + 1, t)

            def x_squares(b):
                for t in range(TT):
                    if b:
                        act.wait_ge(x_squared, 2 * b - 1 + t)
                    act.activation(gated[:, t, :], res[:, t, NG * b:NG * (b + 1)], ACT.Square,
                                   accum_out=ss_x[:, t, b:b + 1]).then_inc(x_squared, 1)

            def par_copy(j):
                act.wait_ge(par_turned, j + 1)
                cols, src = [(slice(0, R_N2), acc[3]), (slice(R_N2, N_PAR), aux[0])][j]
                act.activation(par[:, cols], src[:, 0:cols.stop - cols.start], ACT.Copy).then_inc(par_ready, 1)

            def small_work(n):
                g, c = n // GC, n % GC
                if n in (1, 3, 5):
                    x_hi((n + 1) // 2)
                if n in (2, 4, 6, 7):
                    x_squares((2, 4, 6, 7).index(n))
                if n == 8:
                    act.wait_ge(x_tot, 1)
                    act.wait_ge(const_ready, CONSTS)
                    act.activation(root, tot, ACT.Sqrt, bias=eps, scale=1.0 / D).then_inc(x_root, 1)
                if n == 9:
                    par_copy(1)
                    act.wait_ge(wif_landed, 16)
                    act.activation(w_if_parts[:, :, 0:8], w_if[:], ACT.Copy).then_inc(wif_hi, 1)
                if 1 <= g <= 4 and c == LAG - 1:
                    act.wait_ge(chunk_used, g * GC)
                    banks = acc[2 * ((g - 1) % 2):2 * ((g - 1) % 2) + 2]
                    for t in range(TT):
                        act.activation(gated[:, t, :], banks[t][:], ACT.Square).then_inc(squared, 1)
                if 1 <= g <= 4 and c == LAG:
                    act.wait_ge(qk_var, g)
                    act.activation(qk_root, qk_v, ACT.Sqrt, bias=eps).then_inc(qk_rooted, 1)
                if 1 <= g <= 4 and c == 2 * LAG:
                    dst, w = (aq, R_QN) if g <= 2 else (ak, R_KN)
                    b = 4 * ((g - 1) % 2)
                    for t in range(TT):
                        act.wait_ge(qk_turned, 2 * g - 1 + t)
                        act.activation(dst[:, b:b + 4, P * t:P * (t + 1)],
                                       aux[t][:].rearrange("p (k s) -> p k s", k=4),
                                       ACT.Copy, scale=par[:, w:w + 1]).then_inc(qk_out, 1)
                if 5 <= g <= 10 and c == LAG - 1:
                    act.wait_ge(chunk_used, g * GC)
                    banks = acc[2 * ((g - 1) % 2):2 * ((g - 1) % 2) + 2]
                    for t in range(TT):
                        if g - 1 < G_MQ:
                            o = NG * (g - 1 - G_AV)
                            dst, src, done = av[:, t, o:o + NG], banks[t][:], av_ready
                        elif g - 1 < G_MV:
                            dst, src, done = stage[:, t, :], banks[t][:], stage_ready
                            act.wait_ge(y_turned, 3 if g - 1 == G_MQ else 4)
                        else:
                            o = 2 * (g - 1 - G_MV)
                            dst = mv[:, t, o:o + 2, 0:DV]
                            src, done = banks[t][:].rearrange("p (h d) -> p h d", h=2), mv_ready
                        act.activation(dst, src, ACT.Copy, scale=r1[:, t:t + 1]).then_inc(done, 1)
                if n == AT_GATES + LAG:
                    act.wait_ge(gates_read, 1)
                    act.activation(lam_exp, aux[2][:, 32:34], ACT.Exp).then_inc(lam_exped, 1)
                if n == AT_ROWS + LAG:
                    act.wait_ge(f_ready, 1)
                    then(act.activation(f_exp[:], f_abs[:], ACT.Exp, scale=-1.0))
                    act.activation(f_ln[:], f_exp[:], ACT.Ln, bias=one_col[0:HEADS, :]).then_inc(ln_ready, 1)
                if n == AT_COLS + LAG:
                    act.wait_ge(cols_read, 1)
                    act.activation(exp_nm, aux[2][:, 8:16], ACT.Exp).then_inc(cols_read, 1)
                for h in range(HEADS):
                    if n == AT_SCORE[h] + LAG + 1:
                        act.wait_ge(maxed, h + 1)
                        if h:
                            act.wait_ge(mat_ready, h)
                        for c in range(2):
                            act.activation(probs[:, c, 0:P], aux[1][:, P * c:P * (c + 1)], ACT.Exp,
                                           bias=a_nmax[:, c:c + 1], scale=SCALE, accum_out=a_sum[:, c:c + 1])
                            e = act.activation(probs[:, c, P:P + SEQ], aux[0][:, SEQ * c:SEQ * (c + 1)], ACT.Exp,
                                               bias=a_nmax[:, 2 + c:3 + c], scale=SCALE,
                                               accum_out=a_sum[:, 2 + c:3 + c])
                        e.then_inc(exped, 1)
                    if n == AT_PT[h] + 1:
                        act.wait_ge(mat_turned, h + 1)
                        if h:
                            act.wait_ge(pv_done, h)
                        act.activation(a_turn[:], aux[2][:, 0:P + SEQ], ACT.Copy).then_inc(mat_out, 1)
                    if n == AT_PV[h] + 2:
                        act.wait_ge(pv_done, h + 1)
                        for t in range(TT):
                            s = act.activation(gated[:, t, 0:DV], aux[3][:, DV * t:DV * (t + 1)], ACT.Square,
                                               accum_out=y_ss[:, t:t + 1])
                        then(s)
                        act.activation(y_root, y_ss, ACT.Sqrt, bias=eps, scale=1.0 / DV).then_inc(y_squared, 1)
                        act.wait_ge(y_factor, h + 1)
                        act.wait_ge(qk_turned, 8)
                        if h:
                            act.wait_ge(y_turned, h)
                        if h == HEADS - 1:
                            act.wait_ge(m_turned, 1)
                        for t in range(TT):
                            s = act.activation(stage[:, t, 0:DV], aux[3][:, DV * t:DV * (t + 1)], ACT.Copy,
                                               scale=y_f[:, t:t + 1])
                        s.then_inc(y_scaled, 1)
                    if n == AT_Y[h] + LAG:
                        act.wait_ge(y_mul, h + 1)
                        act.activation(y_hi[:, 8 + 2 * h:10 + 2 * h, :],
                                       scaled[:, 0, :].rearrange("p (k s) -> p k s", k=2),
                                       ACT.Copy).then_inc(y_hi_done, 1)
                if g in (G_MQ + 1, G_MK + 1) and c == 2 * LAG:
                    j = g - G_MQ - 1
                    act.wait_ge(m_turned, j + 1)
                    if j:
                        act.wait_ge(silu_done, j)
                    for b in range(HEADS):
                        act.activation(conv[:, b, :], aux[b // 2][:, SEQ * (b % 2):SEQ * (b % 2 + 1)],
                                       ACT.Identity, bias=par[:, R_CB + 4 * j + b:R_CB + 4 * j + b + 1],
                                       scale=par[:, R_CW + 24 + 4 * j + b:R_CW + 24 + 4 * j + b + 1]
                                       ).then_inc(conv_first, 1)
                if n in (AT_CONV[0] + 2, AT_CONV[1] + 2):
                    j = int(n > AT_CONV[0] + 2)
                    act.wait_ge(conv_done, j + 1)
                    act.activation((mk if j else mq)[:], conv[:], ACT.Silu).then_inc(silu_done, 1)
                for h in range(HEADS):
                    if n == AT_MS[h] + LAG + 1:
                        act.wait_ge(m_masked, h + 1)
                        if h:
                            act.wait_ge(mw_ready, h)
                        act.activation(m_exp[:, 0:SEQ], m_arg[:, 0:SEQ], ACT.Exp, bias=a_col[:, h:h + 1])
                        act.activation(m_exp[:, SEQ:SEQ + P], m_arg[:, SEQ:SEQ + P], ACT.Exp,
                                       bias=a_col[:, 4 + h:5 + h]).then_inc(m_exped, 1)
                    if n == AT_MPV[h] + LAG:
                        for t in range(TT):
                            act.wait_ge(mnum_read, 2 * h + t + 1)
                            if h:
                                act.wait_ge(msq_done, h)
                            s = act.activation(gated[:, t, 0:DV], aux[2 + t][:, 0:DV], ACT.Square,
                                               accum_out=m_ss[:, 4 * t + h:4 * t + h + 1])
                        s.then_inc(msq_done, 1)
                if n == AT_MPV[3] + LAG:
                    act.wait_ge(m_var, 1)
                    act.activation(m_root, m_v2, ACT.Sqrt, bias=eps, scale=1.0 / DV).then_inc(m_rooted, 1)
                if n in (AT_MY[0] - 1, AT_MY[1] - 1):
                    j = int(n > AT_MY[0])
                    act.wait_ge(chunk_used, (G_MO + j + 1) * GC)
                    if j:
                        act.wait_ge(stage_ready, 14)
                    for t in range(TT):
                        act.activation(gated[:, t, :], acc[2 * j + t][:], ACT.Sigmoid,
                                       scale=r1[:, t:t + 1]).then_inc(sig_done, 1)
                if n in (AT_MY[0] + LAG, AT_MY[1] + LAG):
                    j = int(n > AT_MY[0] + LAG)
                    for t in range(TT):
                        turned_hi(y_hi[:, 4 * j:4 * j + 4, P * t:P * (t + 1)], 9 + 2 * j + t, t)

            def x1_squares(g):
                act.wait_ge(x1_ready, 2 * g + 2)
                for t in range(TT):
                    s = act.activation(gated[:, t, :], res[:, t, NG * g:NG * (g + 1)], ACT.Square,
                                       accum_out=ss_x1[:, t, g:g + 1])
                s.then_inc(x1_squared, 1)

            def x1_hi(g):
                for t in range(TT):
                    turned_hi(act_hi[:, 4 * g:4 * g + 4, P * t:P * (t + 1)], 13 + 2 * g + t, t)

            def hidden_hi(i):
                for t in range(TT):
                    act.wait_ge(hid_turned, i * 2 + (t - 1))
                    act.activation(hid_hi[:, bass.ds(i * 4 - 4, 4), P * t:P * (t + 1)],
                                   aux[t][:].rearrange("p (k s) -> p k s", k=4), ACT.Copy).then_inc(hid_hi_done, 1)

            def gate(i, first):
                act.wait_ge(chunk_used, i * FF_CHUNKS + (FF0 + GC))
                if not first:
                    act.wait_ge(hid_ready, i * 2)
                for t in range(TT):
                    act.activation(gated[:, t, :], acc[t][:], ACT.Silu, scale=r2[:, t:t + 1]).then_inc(gate_act, 1)

            par_copy(0)
            for n in range(FF0):
                split_hi(n, n % SPLIT)
                if n == 0:
                    x_hi(0)
                small_work(n)
                if n > OUT0 + GC and (n - OUT0) % GC == LAG - 1:
                    x1_squares((n - OUT0) // GC - 1)
                if n > OUT0 + GC and (n - OUT0) % GC == 2 * LAG:
                    x1_hi((n - OUT0) // GC - 1)

            def ff_slice(i, first):
                for c in range(FF_CHUNKS):
                    split_hi_from(FF0, i * FF_CHUNKS, c)
                    if c == LAG - 1 and first:
                        x1_squares(3)
                    if c == 2 * LAG and first:
                        x1_hi(3)
                        act.wait_ge(x1_tot, 1)
                        act.activation(root, tot, ACT.Sqrt, bias=eps, scale=1.0 / D).then_inc(x1_root, 1)
                    if c == 2 * LAG and not first:
                        hidden_hi(i)
                    if c == GC + LAG - 1:
                        if first:
                            act.wait_ge(r2_ready, 1)
                        gate(i, first)

            ff_slice(0, True)
            with act.Fori(1, FF_SLICES) as i:
                ff_slice(i, False)
            for c in range(2 * SPLIT):
                split_hi(DOWN0 + c, c % SPLIT)
                if c == 2 * LAG:
                    hidden_hi(FF_SLICES)
            with act.Fori(2, 2 * KF // SPLIT) as i:
                for c in range(SPLIT):
                    split_hi_from(DOWN0, i * SPLIT, c)

        @block.vector
        def _(dve):
            steps = [0]

            def then(*instructions):
                for ins in instructions:
                    steps[0] += 1
                    ins.then_inc(dve_step, 1)
                dve.wait_ge(dve_step, steps[0])

            def split_lo(n, slot):
                dve.wait_ge(hi_done, n + 1)
                dve.tensor_tensor(w_lo[:, slot, :], w_raw[:, slot, :], w_hi[:, slot, :].bitcast(F32),
                                  ALU.subtract).then_inc(lo_done, 1)

            counts = {"turns": 0}

            def weighted(banks, w):
                if counts["turns"]:
                    dve.wait_ge(turn_lo, counts["turns"])
                for t in range(TT):
                    dve.wait_ge(turned, counts["turns"] + t + 1)
                    weights = par[:, w:w + 4].unsqueeze(2).to_broadcast([P, 4, P])
                    dve.tensor_tensor(scaled[:, t, :].rearrange("p (k s) -> p k s", k=4),
                                      banks[t][:].rearrange("p (k s) -> p k s", k=4), weights,
                                      ALU.mult).then_inc(scaled_ready, 1)

            def weighted_lo(hi, lo):
                for t in range(TT):
                    counts["turns"] += 1
                    dve.wait_ge(turn_hi, counts["turns"])
                    tok = slice(P * t, P * (t + 1))
                    dve.tensor_tensor(lo[:, :, tok], scaled[:, t, :].rearrange("p (k s) -> p k s", k=4),
                                      hi[:, :, tok].bitcast(F32), ALU.subtract).then_inc(turn_lo, 1)

            def x_weighted(b):
                weighted(aux[2 * (b % 2):2 * (b % 2) + 2], R_N1 + 4 * b)

            def x_lo(b):
                weighted_lo(act_hi[:, 4 * b:4 * b + 4, :], act_lo[:, 4 * b:4 * b + 4, :])

            def small_work(n):
                g, c = n // GC, n % GC
                if n in (1, 3, 5):
                    x_weighted((n + 1) // 2)
                    x_lo((n + 1) // 2)
                if n == 8:
                    dve.wait_ge(x_squared, 8)
                    dve.tensor_reduce(tot, ss_x, AX.X, ALU.add).then_inc(x_tot, 1)
                    dve.wait_ge(x_root, 1)
                    then(dve.reciprocal(r1, root))
                    dve.scalar_tensor_tensor(out=r1sq, in0=r1, scalar=1.0 / DQK, in1=r1, op0=ALU.mult,
                                             op1=ALU.mult).then_inc(r1_ready, 1)
                if n == 9:
                    dve.wait_ge(par_ready, 2)
                    dve.wait_ge(wif_hi, 1)
                    dve.tensor_tensor(w_if_parts[:, :, 8:16], w_if[:], w_if_parts[:, :, 0:8].bitcast(F32), ALU.subtract)
                    dve.tensor_tensor(lam_prod, par[:, R_LAM:R_LAM + 2], par[:, R_LAM + 2:R_LAM + 4],
                                      ALU.mult).then_inc(wif_lo, 1)
                if 1 <= g <= 4 and c == LAG - 1:
                    for t in range(TT):
                        dve.wait_ge(squared, 2 * (g - 1) + t + 1)
                        then(dve.tensor_reduce(qk_ss[:, 4 * t:4 * t + 4],
                                               gated[:, t, :].rearrange("p (h d) -> p h d", h=4), AX.X, ALU.add))
                    dve.wait_ge(r1_ready, 1)
                    for t in range(TT):
                        v = dve.tensor_scalar(qk_v[:, 4 * t:4 * t + 4], qk_ss[:, 4 * t:4 * t + 4],
                                              r1sq[:, t:t + 1], None, ALU.mult)
                    v.then_inc(qk_var, 1)
                if 1 <= g <= 4 and c == LAG + 1:
                    dve.wait_ge(qk_rooted, g)
                    then(dve.reciprocal(qk_f, qk_root))
                    then(dve.tensor_tensor(qk_n, qk_f, qk_f, ALU.mult))
                    then(dve.scalar_tensor_tensor(out=qk_n, in0=qk_v, scalar=EPS, in1=qk_n, op0=ALU.add,
                                                  op1=ALU.mult))
                    then(dve.tensor_scalar(qk_n, qk_n, -0.5, 1.5, ALU.mult, ALU.add))
                    then(*[dve.scalar_tensor_tensor(out=qk_f[:, 4 * t:4 * t + 4], in0=qk_f[:, 4 * t:4 * t + 4],
                                                    scalar=r1[:, t:t + 1], in1=qk_n[:, 4 * t:4 * t + 4],
                                                    op0=ALU.mult, op1=ALU.mult) for t in range(TT)])
                    banks = acc[2 * ((g - 1) % 2):2 * ((g - 1) % 2) + 2]
                    if g >= 2:
                        dve.wait_ge(qk_turned, 2 * (g - 1))
                    for t in range(TT):
                        f = qk_f[:, 4 * t:4 * t + 4].unsqueeze(2).to_broadcast([P, 4, P])
                        dve.tensor_tensor(stage[:, t, :].rearrange("p (h d) -> p h d", h=4),
                                          banks[t][:].rearrange("p (h d) -> p h d", h=4), f,
                                          ALU.mult).then_inc(stage_ready, 1)
                if n == AT_GATES + LAG:
                    dve.wait_ge(gates_done, 1)
                    then(*[dve.tensor_scalar(gate_part[:, t, :], aux[2][:, 16 * t:16 * t + 8], r1[:, t:t + 1],
                                             None, ALU.mult) for t in range(TT)])
                    for t in range(TT):
                        s = dve.scalar_tensor_tensor(out=gate_cols[:, t, :], in0=aux[2][:, 16 * t + 8:16 * t + 16],
                                                     scalar=r1[:, t:t + 1], in1=gate_part[:, t, :],
                                                     op0=ALU.mult, op1=ALU.add)
                    s.then_inc(gates_read, 1)
                    dve.wait_ge(lam_exped, 1)
                    dve.scalar_tensor_tensor(out=neg_lam, in0=lam_exp[:, 1:2], scalar=-LAM_INIT,
                                             in1=lam_exp[:, 0:1], op0=ALU.add, op1=ALU.subtract
                                             ).then_inc(lam_read, 1)
                if n == AT_ROWS + LAG:
                    dve.wait_ge(rows_turned, 1)
                    dve.wait_ge(bias_landed, 32)
                    then(dve.tensor_scalar(f_pre[:], aux[3][0:HEADS, SEQ:2 * SEQ], bias_if[:, 1:2], None, ALU.add))
                    dve.scalar_tensor_tensor(out=f_abs[:], in0=f_pre[:], scalar=-1.0, in1=f_pre[:],
                                             op0=ALU.mult, op1=ALU.max).then_inc(f_ready, 1)
                    dve.wait_ge(ln_ready, 1)
                    then(dve.scalar_tensor_tensor(out=log_f[:], in0=f_pre[:], scalar=0.0, in1=f_ln[:],
                                                  op0=ALU.min, op1=ALU.subtract))
                    then(dve.tensor_tensor_scan(f_sum[:], log_f[:], zero_row[:], 0.0, ALU.add, ALU.add))
                    then(dve.scalar_tensor_tensor(out=a_row[:], in0=aux[3][0:HEADS, 0:SEQ],
                                                  scalar=bias_if[:, 0:1], in1=f_sum[:], op0=ALU.add,
                                                  op1=ALU.subtract))
                    then(dve.tensor_tensor_scan(m_run[:], a_row[:], a_row[:], NEG, ALU.max, ALU.max))
                    dve.tensor_scalar(neg_run[:], m_run[:], -1.0, None, ALU.mult)
                    dve.scalar_tensor_tensor(out=neg_m[:], in0=f_sum[:], scalar=-1.0, in1=m_run[:],
                                             op0=ALU.mult, op1=ALU.subtract).then_inc(rows_ready, 1)
                if n == AT_COLS + LAG:
                    dve.wait_ge(cols_turned, 1)
                    dve.tensor_copy(a_col, aux[2][:, 0:8]).then_inc(cols_read, 1)
                for h in range(HEADS):
                    if n == AT_SCORE[h] + LAG:
                        dve.wait_ge(scored, h + 1)
                        t0 = aux[1][:, 0:SEQ].rearrange("p (c k) -> p c k", c=2)
                        t1 = aux[0][:].rearrange("p (c k) -> p c k", c=2)
                        then(dve.tensor_tensor(t0[:, :, 64:P], t0[:, :, 64:P], chunk_mask[:], ALU.add),
                             dve.tensor_tensor(t1[:, :, 192:SEQ], t1[:, :, 192:SEQ], chunk_mask[:], ALU.add))
                        then(dve.tensor_reduce(a_max[:, 0:2], t0, AX.X, ALU.max),
                             dve.tensor_reduce(a_max[:, 2:4], t1, AX.X, ALU.max))
                        dve.tensor_scalar(a_nmax, a_max, -SCALE, None, ALU.mult).then_inc(maxed, 1)
                    if n == AT_SCORE[h] + LAG + 1:
                        dve.wait_ge(exped, h + 1)
                        then(dve.reciprocal(a_rec, a_sum))
                        then(*[dve.tensor_scalar(a_mix[:, t:t + 1], a_rec[:, 2 * t + 1:2 * t + 2], neg_lam,
                                                 None, ALU.mult) for t in range(TT)])
                        then(*[dve.tensor_scalar(a_tmp[:, parts[t]], probs[:, 1, parts[t]], a_mix[:, t:t + 1],
                                                 None, ALU.mult) for t in range(TT)])
                        if h:
                            dve.wait_ge(mat_turned, h)
                        for t in range(TT):
                            m = dve.scalar_tensor_tensor(out=a_mat[:, parts[t]], in0=probs[:, 0, parts[t]],
                                                         scalar=a_rec[:, 2 * t:2 * t + 1], in1=a_tmp[:, parts[t]],
                                                         op0=ALU.mult, op1=ALU.add)
                        m.then_inc(mat_ready, 1)
                    if n == AT_PV[h] + 2:
                        dve.wait_ge(y_squared, h + 1)
                        then(dve.reciprocal(y_rec, y_root))
                        dve.tensor_scalar(y_f, y_rec, 1.0 - LAM_INIT, None, ALU.mult).then_inc(y_factor, 1)
                    if n == AT_Y[h] + LAG:
                        dve.wait_ge(y_turned, h + 1)
                        w = par[:, R_AN + 2 * h:R_AN + 2 * h + 2].unsqueeze(2).to_broadcast([P, 2, SEQ])
                        dve.tensor_tensor(scaled[:, 0, :].rearrange("p (k s) -> p k s", k=2),
                                          aux[3][:].rearrange("p (k s) -> p k s", k=2), w,
                                          ALU.mult).then_inc(y_mul, 1)
                        dve.wait_ge(y_hi_done, h + 1)
                        ks = slice(8 + 2 * h, 10 + 2 * h)
                        dve.tensor_tensor(y_lo[:, ks, :], scaled[:, 0, :].rearrange("p (k s) -> p k s", k=2),
                                          y_hi[:, ks, :].bitcast(F32), ALU.subtract).then_inc(y_lo_done, 1)
                for j, start in enumerate(AT_CONV):
                    if n in (start, start + 1, start + 2):
                        shift = n - start + 1
                        for b in range(HEADS):
                            if shift == 1:
                                dve.wait_ge(conv_first, 4 * j + 2 * (b // 2) + 2)
                            w = R_CW + 8 * (CONV_W - 1 - shift) + 4 * j + b
                            o = SEQ * (b % 2)
                            tap = dve.scalar_tensor_tensor(
                                out=conv[:, b, shift:SEQ], in0=aux[b // 2][:, o:o + SEQ - shift],
                                scalar=par[:, w:w + 1], in1=conv[:, b, shift:SEQ], op0=ALU.mult, op1=ALU.add)
                            if shift < CONV_W - 1:
                                steps[0] += 1
                                tap.then_inc(dve_step, 1)
                        if shift < CONV_W - 1:
                            dve.wait_ge(dve_step, steps[0])
                    if n == start + 2:
                        tap.then_inc(conv_done, 1)
                for h in range(HEADS):
                    if n == AT_MS[h] + LAG:
                        dve.wait_ge(m_scored, h + 1)
                        dve.tensor_tensor(m_arg[:, 0:SEQ], aux[1][:, 0:SEQ], causal[:], ALU.add)
                        dve.tensor_tensor(m_arg[:, SEQ:SEQ + P], aux[1][:, P:SEQ], causal[:, 0:P],
                                          ALU.add).then_inc(m_masked, 1)
                    if n == AT_MS[h] + LAG + 1:
                        dve.wait_ge(m_exped, h + 1)
                        if h:
                            dve.wait_ge(mpv_done, h)
                        dve.scalar_tensor_tensor(out=m_w[:], in0=aux[0][:, 0:P + SEQ], scalar=SCALE, in1=m_exp[:],
                                                 op0=ALU.mult, op1=ALU.mult).then_inc(mw_ready, 1)
                    if n == AT_MPV[h] + LAG:
                        dve.wait_ge(mpv_done, h + 1)
                        for t in range(TT):
                            dve.tensor_copy(m_num[:, t, h, :], aux[2 + t][:, 0:DV + 1]).then_inc(mnum_read, 1)
                if n == AT_MPV[3] + LAG:
                    dve.wait_ge(mnum_read, 8)
                    dve.wait_ge(msq_done, 4)
                    den = m_num[:, :, :, DV:DV + 1].rearrange("p t h o -> p t (h o)")
                    den8 = m_den.rearrange("p (t h) -> p t h", t=TT)
                    then(dve.scalar_tensor_tensor(out=den8, in0=den, scalar=-1.0, in1=den, op0=ALU.mult,
                                                  op1=ALU.max))
                    then(dve.tensor_tensor(m_den, m_den, exp_nm, ALU.max))
                    then(dve.reciprocal(m_rec, m_den))
                    then(dve.tensor_tensor(m_v, m_ss, m_rec, ALU.mult))
                    dve.tensor_tensor(m_v2, m_v, m_rec, ALU.mult).then_inc(m_var, 1)
                    dve.wait_ge(m_rooted, 1)
                    then(dve.reciprocal(m_v, m_root))
                    then(dve.tensor_tensor(m_rec, m_rec, m_v, ALU.mult))
                if n in (AT_MY[0] - 1, AT_MY[1] - 1):
                    j = int(n > AT_MY[0])
                    if j:
                        dve.wait_ge(turned, 10)
                    else:
                        dve.wait_ge(m_turned, 2)
                    for t in range(TT):
                        dve.wait_ge(sig_done, 2 * j + t + 1)
                        for b in range(2):
                            h = 2 * j + b
                            s = dve.scalar_tensor_tensor(
                                out=stage[:, t, DV * b:DV * (b + 1)], in0=m_num[:, t, h, 0:DV],
                                scalar=m_rec[:, 4 * t + h:4 * t + h + 1], in1=gated[:, t, DV * b:DV * (b + 1)],
                                op0=ALU.mult, op1=ALU.mult)
                        s.then_inc(stage_ready, 1)
                if n in (AT_MY[0] + LAG, AT_MY[1] + LAG):
                    j = int(n > AT_MY[0] + LAG)
                    weighted(aux[0:2], R_MN + 4 * j)
                    weighted_lo(y_hi[:, 4 * j:4 * j + 4, :], y_lo[:, 4 * j:4 * j + 4, :])

            def free_group(n):
                g, c = n // GC, n % GC
                if 1 <= g <= len(IN_COLS) and c == LAG + 2:
                    last = {G_AQ: (stage_ready, 2), G_AQ + 1: (stage_ready, 4), G_AK: (stage_ready, 6),
                            G_AK + 1: (stage_ready, 8), G_AV: (av_ready, 2), G_AV + 1: (av_ready, 4),
                            G_MQ: (stage_ready, 10), G_MK: (stage_ready, 12), G_MV: (mv_ready, 2),
                            G_MV + 1: (mv_ready, 4), G_MO: (sig_done, 2), G_MO + 1: (sig_done, 4)}[g - 1]
                    dve.wait_ge(*last)
                    dve.sem_inc(acc_free, 1)

            def x1_group(g):
                dve.wait_ge(chunk_used, OUT0 + (g + 1) * GC)
                for t in range(TT):
                    r = res[:, t, NG * g:NG * (g + 1)]
                    dve.tensor_tensor(r, r, acc[2 * (g % 2) + t][:], ALU.add).then_inc(x1_ready, 1)

            def x1_block(g):
                weighted(aux[0:2], R_N2 + 4 * g)
                weighted_lo(act_hi[:, 4 * g:4 * g + 4, :], act_lo[:, 4 * g:4 * g + 4, :])

            def hidden(i):
                dve.wait_ge(chunk_used, i * FF_CHUNKS + FF0)
                dve.wait_ge(gate_act, i * 2)
                for t in range(TT):
                    dve.scalar_tensor_tensor(out=stage[:, t, :], in0=acc[2 + t][:], scalar=r2[:, t:t + 1],
                                             in1=gated[:, t, :], op0=ALU.mult, op1=ALU.mult).then_inc(hid_ready, 1)

            def hidden_lo(i):
                for t in range(TT):
                    dve.wait_ge(hid_hi_done, i * 2 + (t - 1))
                    ks, tok = bass.ds(i * 4 - 4, 4), slice(P * t, P * (t + 1))
                    dve.tensor_tensor(hid_lo[:, ks, tok], aux[t][:].rearrange("p (k s) -> p k s", k=4),
                                      hid_hi[:, ks, tok].bitcast(F32), ALU.subtract).then_inc(hid_lo_done, 1)

            for n in range(FF0):
                if n == 0:
                    dve.wait_ge(par_ready, 1)
                    x_weighted(0)
                split_lo(n, n % SPLIT)
                if n == 0:
                    x_lo(0)
                small_work(n)
                free_group(n)
                if n > OUT0 + GC and (n - OUT0) % GC == LAG - 1:
                    x1_group((n - OUT0) // GC - 1)
                if n > OUT0 + GC and (n - OUT0) % GC == 2 * LAG:
                    x1_block((n - OUT0) // GC - 1)

            def ff_slice(i, first):
                for c in range(FF_CHUNKS):
                    split_lo(i * FF_CHUNKS + (FF0 + c), c % SPLIT)
                    if first and c == LAG - 1:
                        x1_group(3)
                    if first and c == 2 * LAG:
                        x1_block(3)
                        dve.wait_ge(x1_squared, 4)
                        dve.tensor_reduce(tot, ss_x1, AX.X, ALU.add).then_inc(x1_tot, 1)
                        dve.wait_ge(x1_root, 1)
                        dve.reciprocal(r2, root).then_inc(r2_ready, 1)
                        dve.wait_ge(r2_ready, 1)
                    if not first and c == LAG - 1:
                        hidden(i)
                    if not first and c == 2 * LAG:
                        hidden_lo(i)

            ff_slice(0, True)
            with dve.Fori(1, FF_SLICES) as i:
                ff_slice(i, False)

            def output(p):
                banks = [[acc[0], acc[1], aux[2], aux[3]], [acc[2], acc[3], aux[0], aux[1]]][p]
                for j in range(4):
                    if p:
                        dve.wait_ge(bank_done, j + 1)
                    else:
                        dve.wait_ge(chunk_used, DOWN0 + KF)
                    col, t = CH * p + NG * (j // 2), j % 2
                    r = res[:, t, col:col + NG]
                    dve.tensor_tensor(r, r, banks[j][:], ALU.add).then_inc(out_ready, 1)

            for c in range(2 * SPLIT):
                split_lo(DOWN0 + c, c % SPLIT)
                if c == LAG - 1:
                    hidden(FF_SLICES)
                if c == 2 * LAG:
                    hidden_lo(FF_SLICES)
            with dve.Fori(2, KF // SPLIT) as i:
                for c in range(SPLIT):
                    split_lo(i * SPLIT + (DOWN0 + c), c)
            for c in range(SPLIT):
                split_lo(DOWN0 + KF + c, c)
                if c == LAG - 1:
                    output(0)
            with dve.Fori(KF // SPLIT + 1, 2 * KF // SPLIT) as i:
                for c in range(SPLIT):
                    split_lo(i * SPLIT + (DOWN0 + c), c)
            output(1)


_INS = ['x', 'norm1_w', 'w_in', 'conv_w', 'conv_b', 'i_bias', 'f_bias', 'm_norm_w', 'q_norm_w', 'k_norm_w',
        'lambda_q1', 'lambda_k1', 'lambda_q2', 'lambda_k2', 'a_norm_w', 'w_out', 'norm2_w', 'w_gate',
        'w_up', 'w_down']


def kernel(**inputs):
    import concourse.bacc as bacc
    from concourse.bass_utils import run_bass_kernel_spmd

    nc = bacc.Bacc("TRN2", target_bir_lowering=False, num_devices=1)
    arrays, args = {}, []
    for name in _INS:
        a = np.ascontiguousarray(inputs[name])
        arrays[f"in_{name}"] = a
        args.append(nc.dram_tensor(f"in_{name}", a.shape, mybir.dt.from_np(a.dtype), kind="ExternalInput").ap())
    args.append(nc.dram_tensor("out_0", (1, SEQ, D), F32, kind="ExternalOutput").ap())
    hybrid_block_kernel(nc, *args)
    r = run_bass_kernel_spmd(nc, [arrays], core_ids=[0])
    return r.results[0]["out_0"]
```
